# Optimizing a Trainium2 kernel written in Bass

```python
import math
import jax, jax.numpy as jnp
from jax import lax
import numpy as np

D_MODEL = 1024
BATCH = 1
SEQ = 2048
DEPTH = 2

GRID_W = 64
CTX_LEN = 256
N_MIXERS = 2
N_A = (DEPTH + 1) // 2
N_B = DEPTH // 2
N_HEADS = 8
NOPE_DIM = 128
ROPE_DIM = 64
V_DIM = 128
Q_LORA = 384
KV_LORA = 256
ATTN_W = N_HEADS * V_DIM
MLA_IN = Q_LORA + KV_LORA + ROPE_DIM + ATTN_W
ROPE_BASE = 10000.0
Q_BLOCK = 128
CONV_W = D_MODEL
CONV_K = 31
CONV_PAD = CONV_K // 2
EPS = 1e-6

kernel_name = "hybrid_mla_conformer_prefix_dit"

def rms_norm(x, g):
    xf = x.astype(jnp.float32)
    y = xf * lax.rsqrt(jnp.mean(xf * xf, axis=-1, keepdims=True) + EPS)
    return (y * g.astype(jnp.float32)).astype(x.dtype)

def layer_norm(x, g, b):
    xf = x.astype(jnp.float32)
    mu = jnp.mean(xf, axis=-1, keepdims=True)
    var = jnp.mean(jnp.square(xf - mu), axis=-1, keepdims=True)
    y = (xf - mu) * lax.rsqrt(var + EPS)
    return (y * g.astype(jnp.float32) + b.astype(jnp.float32)).astype(x.dtype)

def axial_rope_tables(n_tokens, dtype):
    rows_n = n_tokens // GRID_W
    rows = jnp.repeat(jnp.arange(rows_n, dtype=jnp.float32), GRID_W)
    cols = jnp.tile(jnp.arange(GRID_W, dtype=jnp.float32), rows_n)
    half = ROPE_DIM // 2
    freqs = 1.0 / (ROPE_BASE ** (jnp.arange(0, half, 2, dtype=jnp.float32) / half))
    ang_r = rows[:, None] * freqs[None, :]
    ang_c = cols[:, None] * freqs[None, :]
    return tuple(t.astype(dtype) for t in (jnp.cos(ang_r), jnp.sin(ang_r), jnp.cos(ang_c), jnp.sin(ang_c)))

def _rotate(x, cos, sin):
    x1, x2 = jnp.split(x, 2, axis=-1)
    return jnp.concatenate([x1 * cos - x2 * sin, x1 * sin + x2 * cos], axis=-1)

def rope_2d(x, tables):
    cr, sr, cc, sc = tables
    xr, xc = jnp.split(x, 2, axis=-1)
    return jnp.concatenate([_rotate(xr, cr, sr), _rotate(xc, cc, sc)], axis=-1)

def mla_qkv(h, w_in, g_q, w_uq, g_kv, w_ukv, tables):
    b, l, _ = h.shape
    u = h @ w_in
    cq, ckv, kr, gate = jnp.split(u, [Q_LORA, Q_LORA + KV_LORA, Q_LORA + KV_LORA + ROPE_DIM], axis=-1)
    q = (rms_norm(cq, g_q) @ w_uq).reshape(b, l, N_HEADS, NOPE_DIM + ROPE_DIM).transpose(0, 2, 1, 3)
    kv = (rms_norm(ckv, g_kv) @ w_ukv).reshape(b, l, N_HEADS, NOPE_DIM + V_DIM).transpose(0, 2, 1, 3)
    k_nope, v = jnp.split(kv, [NOPE_DIM], axis=-1)
    q_nope, q_rope = jnp.split(q, [NOPE_DIM], axis=-1)
    if tables is not None:
        q_rope = rope_2d(q_rope, tables)
        kr = rope_2d(kr, tables)
    k_rope = jnp.broadcast_to(kr[:, None], (b, N_HEADS, l, ROPE_DIM))
    q = jnp.concatenate([q_nope, q_rope], axis=-1)
    k = jnp.concatenate([k_nope, k_rope], axis=-1)
    return q, k, v, gate

def block_attention(q, k, v):
    b, h, lq, dq = q.shape
    dv = v.shape[-1]
    nb = lq // Q_BLOCK
    scale = 1.0 / math.sqrt(dq)
    qb = q.reshape(b, h, nb, Q_BLOCK, dq).transpose(2, 0, 1, 3, 4)

    def one_block(qi):
        s = jnp.einsum('bhqd,bhkd->bhqk', qi, k).astype(jnp.float32) * scale
        p = jax.nn.softmax(s, axis=-1).astype(v.dtype)
        return jnp.einsum('bhqk,bhkd->bhqd', p, v)

    o = lax.map(one_block, qb)
    return o.transpose(1, 0, 3, 2, 4).reshape(b, lq, h * dv)

def conformer_conv_branch(h, w_in, w_dw, b_dw, g_ln, b_ln, w_o):
    a, bgl, g = jnp.split(h @ w_in, 3, axis=-1)
    u = a * jax.nn.sigmoid(bgl)
    u = lax.conv_general_dilated(u, w_dw, window_strides=(1,), padding=[(CONV_PAD, CONV_PAD)],
                                 dimension_numbers=('NWC', 'WIO', 'NWC'),
                                 feature_group_count=CONV_W) + b_dw
    u = jax.nn.silu(layer_norm(u, g_ln, b_ln)) * jax.nn.silu(g)
    return u @ w_o

def setup_inputs(seed: int = 0) -> dict:
    key = jax.random.key(seed)
    ks = iter(jax.random.split(key, 32))
    f32 = jnp.float32

    def nrm(shape, scale):
        return jax.random.normal(next(ks), shape, f32) * scale

    d = D_MODEL
    return {
        "x": nrm((BATCH, SEQ, d), 1.0),
        "c": nrm((BATCH, d), 1.0),
        "ctx": nrm((BATCH, CTX_LEN, d), 1.0),
        "c_ctx": nrm((d,), 1.0),
        "w_mod": nrm((DEPTH, d, 3 * d), 0.3 * d ** -0.5),
        "b_mod": nrm((DEPTH, 3 * d), 0.01),
        "g_pre": 1.0 + nrm((DEPTH, d), 0.02),
        "g_post": 1.0 + nrm((DEPTH, d), 0.02),
        "mla_w_in": nrm((N_A, d, MLA_IN), d ** -0.5),
        "mla_g_q": 1.0 + nrm((N_A, Q_LORA), 0.02),
        "mla_w_uq": nrm((N_A, Q_LORA, N_HEADS * (NOPE_DIM + ROPE_DIM)), Q_LORA ** -0.5),
        "mla_g_kv": 1.0 + nrm((N_A, KV_LORA), 0.02),
        "mla_w_ukv": nrm((N_A, KV_LORA, N_HEADS * (NOPE_DIM + V_DIM)), KV_LORA ** -0.5),
        "mla_w_o": nrm((N_A, ATTN_W, d), ATTN_W ** -0.5),
        "cv_w_in": nrm((N_B, d, 3 * CONV_W), d ** -0.5),
        "cv_w_dw": nrm((N_B, CONV_K, 1, CONV_W), CONV_K ** -0.5),
        "cv_b_dw": nrm((N_B, CONV_W), 0.01),
        "cv_g_ln": 1.0 + nrm((N_B, CONV_W), 0.02),
        "cv_b_ln": nrm((N_B, CONV_W), 0.01),
        "cv_w_o": nrm((N_B, CONV_W, d), CONV_W ** -0.5),
    }

def reference(x, c, ctx, c_ctx, w_mod, b_mod, g_pre, g_post,
              mla_w_in, mla_g_q, mla_w_uq, mla_g_kv, mla_w_ukv, mla_w_o,
              cv_w_in, cv_w_dw, cv_b_dw, cv_g_ln, cv_b_ln, cv_w_o):
    b, s, d = x.shape
    tables = axial_rope_tables(s, x.dtype)
    sc = jax.nn.silu(c)
    sc_ctx = jax.nn.silu(c_ctx)

    for i in range(DEPTH):
        last = i == DEPTH - 1
        j = i // N_MIXERS
        shift_x, scale_x, gate_x = jnp.split((sc @ w_mod[i] + b_mod[i])[:, None, :], 3, axis=-1)
        shift_c, scale_c, gate_c = jnp.split(sc_ctx @ w_mod[i] + b_mod[i], 3, axis=-1)
        hx = rms_norm(x, g_pre[i]) * (1.0 + scale_x) + shift_x
        hc = rms_norm(ctx, g_pre[i]) * (1.0 + scale_c) + shift_c

        if i % N_MIXERS == 0:
            qx, kx, vx, gx = mla_qkv(hx, mla_w_in[j], mla_g_q[j], mla_w_uq[j], mla_g_kv[j], mla_w_ukv[j], tables)
            qc, kc, vc, gc = mla_qkv(hc, mla_w_in[j], mla_g_q[j], mla_w_uq[j], mla_g_kv[j], mla_w_ukv[j], None)
            ox = block_attention(qx, jnp.concatenate([kx, kc], axis=2), jnp.concatenate([vx, vc], axis=2))
            yx = (ox * jax.nn.silu(gx)) @ mla_w_o[j]
            if not last:
                oc = block_attention(qc, kc, vc)
                yc = (oc * jax.nn.silu(gc)) @ mla_w_o[j]
        else:
            yx = conformer_conv_branch(hx, cv_w_in[j], cv_w_dw[j], cv_b_dw[j], cv_g_ln[j], cv_b_ln[j], cv_w_o[j])
            if not last:
                yc = conformer_conv_branch(hc, cv_w_in[j], cv_w_dw[j], cv_b_dw[j], cv_g_ln[j], cv_b_ln[j], cv_w_o[j])

        x = x + gate_x * rms_norm(yx, g_post[i])
        if not last:
            ctx = ctx + gate_c * rms_norm(yc, g_post[i])

    return x


_drawn_inputs = setup_inputs


def setup_inputs(seed=0):
    import zlib

    import numpy as np

    out = dict(_drawn_inputs(seed))
    spreads = {}
    factors = {'ctx': 5.01,
     'c_ctx': 3.106,
     'b_mod': 3.262,
     'g_pre': 8.0,
     'g_post': 8.0,
     'mla_g_q': 8.0,
     'mla_g_kv': 8.0,
     'cv_b_dw': 46.778,
     'cv_g_ln': 35.909,
     'cv_b_ln': 64.0}
    for name, (base, spread) in spreads.items():
        noise = np.random.default_rng([zlib.crc32(name.encode()), seed]).standard_normal(out[name].shape)
        drawn = base * np.exp(spread * noise) if base else spread * noise
        out[name] = __import__('jax').numpy.asarray(drawn.astype(out[name].dtype))
    for name, factor in factors.items():
        out[name] = (out[name] * factor).astype(out[name].dtype)
    return out
```

```python
from contextlib import ExitStack

import numpy as np

import concourse.bass as bass
from concourse import mybir

F32 = mybir.dt.float32
F32R = mybir.dt.float32r
ALU = mybir.AluOpType
ACT = mybir.ActivationFunctionType
AXX = mybir.AxisListType.X

P = 128
D = 1024
KD = D // P
SEQ, CTX = 2048, 256
TOK = SEQ + CTX
BLK = 512
NBLK = SEQ // BLK
HEADS, NOPE, ROPE, VDIM = 8, 128, 64, 128
QL, KVL = 384, 256
KQ, KKV = QL // P, KVL // P
CONV_K, PAD = 31, 15
PHASES = 8
CCH = P // PHASES
NCOL = SEQ // PHASES
OFFS = 5
EPS = 1e-6
GRID_W = 64
SCALE = (NOPE + ROPE) ** -0.5
NKT = TOK // P
NCHUNK = 5
SLOTS = NKT + 1


def chunk(c):
    return slice(c * BLK, min((c + 1) * BLK, TOK))


class Chain:

    def __init__(self, eng, sem, base=0):
        self.eng, self.sem, self.base, self.n = eng, sem, base, 0

    def __call__(self, ins):
        self.n += 1
        ins.then_inc(self.sem, 1)
        self.eng.wait_ge(self.sem, self.base + self.n)


class Net:

    def __init__(self, nc, stack):
        self.nc, self.stack = nc, stack

    def sem(self, name):
        return self.nc.alloc_semaphore(name=name)

    def sems(self, name, n):
        return [self.sem(f"{name}{i}") for i in range(n)]


def root_mean(nc, net, out, sums, n):
    return nc.scalar.activation(out, sums, ACT.Sqrt, scale=1.0 / n, bias=net.eps[:])


def split3(nc, out, whi, wlo, xhi, xlo, first, last):
    nc.tensor.matmul(out, whi, xhi, start=first, stop=False)
    nc.tensor.matmul(out, whi, xlo, start=False, stop=False)
    return nc.tensor.matmul(out, wlo, xhi, start=False, stop=last)


def modulation(nc, net):
    R = 4
    tiles = 2 * 3 * KD
    with nc.cleanup_on_exit(), ExitStack() as st:
        sb = lambda n, s, d=F32: st.enter_context(nc.sbuf_tensor(n, s, d))
        wst = sb("mod_w", [P, R, KD, P])
        cc = sb("mod_c", [P, KD, 2])
        csig = sb("mod_csig", [P, KD, 2])
        bm = sb("mod_b", [P, tiles])
        gpre = sb("mod_gpre", [P, 2, KD])
        gpost = sb("mod_gpost", [P, 2, KD])
        gp = sb("mod_gp", [P, 2 * KD])
        gpT = sb("mod_gpT", [2 * KD, P])
        acc = st.enter_context(nc.psum_tensor("mod_acc", [P, BLK], F32))
        accT = st.enter_context(nc.psum_tensor("mod_accT", [P, BLK], F32))
        s_small = net.sem("mod_small")
        s_w = net.sems("mod_w_in", R)
        s_sig, s_silu, s_used, s_all, s_chain, s_gp, s_gpT, s_row, s_out = (
            net.sem("mod_" + n) for n in ("sig", "silu", "used", "all", "chain", "gp", "gpt", "row", "out"))
        mod = net.mod
        accv = acc[:, 0:2 * tiles].rearrange("p (m s) -> p m s", s=2)
        block = st.enter_context(nc.Block())

        @block.sync
        def _(sp):
            for dst, src in ((cc, net.c_cols), (bm, net.b_mod), (gpre, net.g_pre), (gpost, net.g_post),
                             (net.ident, net.ident_in), (net.perm, net.perm_in)):
                sp.dma_start(dst[:], src).then_inc(s_small, 16)
            for r in range(R):
                sp.dma_start(wst[:, r], net.w_mod[r]).then_inc(s_w[r], 16)
            with sp.Fori(0, tiles // R - 1) as i:
                for r in range(R):
                    sp.wait_ge(s_used, i * R + (r + 1))
                    sp.dma_start(wst[:, r], net.w_mod[bass.ds(i * R + (R + r), 1)].rearrange("a p k c -> p (a k) c")
                                 ).then_inc(s_w[r], 16)
            sp.wait_ge(s_row, 1)
            sp.dma_start(net.gp_row, gpT[:]).then_inc(s_out, 16)
            sp.wait_ge(s_out, 16)

        @block.scalar
        def _(act):
            act.wait_ge(s_small, 96)
            nc.scalar.activation(csig[:], cc[:], ACT.Sigmoid).then_inc(s_sig, 1)

        @block.tensor
        def _(pe):
            pe.wait_ge(s_silu, 1)
            with pe.Fori(0, tiles // R) as i:
                for r in range(R):
                    pe.wait_ge(s_w[r], (i + 1) * 16)
                    for k in range(KD):
                        mm = nc.tensor.matmul(acc[:, bass.ds(i * (2 * R) + 2 * r, 2)], wst[:, r, k, :],
                                              cc[:, k, :], start=(k == 0), stop=(k == KD - 1))
                    mm.then_inc(s_used, 1)
            pe.wait_ge(s_gp, 2)
            nc.tensor.transpose(accT[0:2 * KD, 0:P], gp[:], net.ident[:]).then_inc(s_gpT, 1)

        @block.vector
        def _(dve):
            nc.vector.memset(net.eps[:], EPS)
            nc.vector.memset(net.ones[:], 1.0).then_inc(s_all, 1)
            link = Chain(dve, s_chain)
            dve.wait_ge(s_small, 96)
            dve.wait_ge(s_sig, 1)
            nc.vector.tensor_tensor(cc[:], cc[:], csig[:], ALU.mult).then_inc(s_silu, 1)
            dve.wait_ge(s_used, tiles)
            link(nc.vector.tensor_tensor(mod[:], accv, bm[:].unsqueeze(2).to_broadcast([P, tiles, 2]), ALU.add))
            for l in range(2):
                shift = 3 * KD * l
                link(nc.vector.scalar_tensor_tensor(
                    out=net.amul[:, l], in0=mod[:, shift + KD:shift + 2 * KD, :], scalar=1.0,
                    in1=gpre[:, l].unsqueeze(2).to_broadcast([P, KD, 2]), op0=ALU.add, op1=ALU.mult))
                nc.vector.tensor_tensor(gp[:, l * KD:(l + 1) * KD], mod[:, shift + 2 * KD:shift + 3 * KD, 0],
                                        gpost[:, l], ALU.mult).then_inc(s_gp, 1)
            dve.wait_ge(s_gpT, 1)
            nc.vector.tensor_copy(gpT[:], accT[0:2 * KD, 0:P]).then_inc(s_row, 1)


def hidden(nc, net, layer, x_dram, ctx_dram, hhi, hlo):
    tag = f"hid{layer}_"
    R = BLK // P
    with nc.cleanup_on_exit(), ExitStack() as st:
        sb = lambda n, s, d=F32: st.enter_context(nc.sbuf_tensor(tag + n, s, d))
        xt = sb("x", [P, R, D])
        junk = sb("junk", [P, D])
        tmp = sb("tmp", [P, 2, BLK])
        ss = sb("ss", [P, R])
        rs = sb("rs", [P, R])
        ps = st.enter_context(nc.psum_tensor(tag + "ps", [P, KD, BLK], F32))
        s_x = net.sems(tag + "x_in", R)
        s_ss, s_rt, s_rs, s_xr, s_tile, s_tr, s_h, s_hi, s_lo = (
            net.sem(tag + n) for n in ("ss", "rt", "rs", "xr", "tile", "tr", "h", "hi", "lo"))
        mod, amul = net.mod, net.amul
        block = st.enter_context(nc.Block())
        ctx_tiles = CTX // P if ctx_dram is not None else 0

        @block.sync
        def _(sp):
            for r in range(R):
                sp.dma_start(xt[:, r], x_dram[r * P:(r + 1) * P, :]).then_inc(s_x[r], 16)
            with sp.Fori(1, NBLK) as b:
                for r in range(R):
                    if r < R - 1:
                        sp.wait_ge(s_tile, (b - 1) * (R - 1) + (r + 1))
                    else:
                        sp.wait_ge(s_tr, b * KD)
                    sp.dma_start(xt[:, r], x_dram[bass.ds(b * BLK + r * P, P), :]).then_inc(s_x[r], 16)
            for r in range(ctx_tiles):
                sp.wait_ge(s_tile, (NBLK - 1) * (R - 1) + r + 1)
                sp.dma_start(xt[:, r], ctx_dram[r * P:(r + 1) * P, :]).then_inc(s_x[r], 16)

        def act_block(act, b, tiles, stream, width, first=False):
            for r in range(tiles):
                act.wait_ge(s_x[r], (b + 1) * 16)
                nc.scalar.activation(junk[:], xt[:, r], ACT.Square, accum_out=ss[:, r:r + 1]).then_inc(s_ss, 1)
                act.wait_ge(s_ss, b * R + (r + 1))
                root_mean(nc, net, rs[:, r:r + 1], ss[:, r:r + 1], D).then_inc(s_rt, 1)
            for k in range(KD):
                act.wait_ge(s_tr, b * KD + (k + 1))
                if not first or k >= 2:
                    act.wait_ge(s_lo, b * KD + (k - 1))
                nc.scalar.activation(tmp[:, k % 2, 0:width], ps[:, k, 0:width], ACT.Identity,
                                     scale=amul[:, layer, k, stream:stream + 1],
                                     bias=mod[:, 3 * KD * layer + k, stream:stream + 1]).then_inc(s_h, 1)

        @block.scalar
        def _(act):
            act_block(act, 0, R, 0, BLK, True)
            with act.Fori(1, NBLK) as b:
                act_block(act, b, R, 0, BLK)
            if ctx_tiles:
                act_block(act, NBLK, ctx_tiles, 1, CTX)

        def dve_block(dve, b, tiles, stream, width):
            for r in range(tiles):
                dve.wait_ge(s_rt, b * R + (r + 1))
                nc.vector.reciprocal(rs[:, r:r + 1], rs[:, r:r + 1]).then_inc(s_rs, 1)
                dve.wait_ge(s_rs, b * R + (r + 1))
                nc.vector.tensor_scalar(xt[:, r], xt[:, r], rs[:, r:r + 1], None, ALU.mult).then_inc(s_xr, 1)
            for k in range(KD):
                h, l = (t[:, k, bass.ds(b * BLK, width)] for t in (hhi, hlo))
                dve.wait_ge(s_h, b * KD + (k + 1))
                nc.vector.tensor_copy(h, tmp[:, k % 2, 0:width]).then_inc(s_hi, 1)
                dve.wait_ge(s_hi, b * KD + (k + 1))
                nc.vector.tensor_tensor(l, tmp[:, k % 2, 0:width], h.bitcast(F32), ALU.subtract).then_inc(s_lo, 1)

        @block.vector
        def _(dve):
            with dve.Fori(0, NBLK) as b:
                dve_block(dve, b, R, 0, BLK)
            if ctx_tiles:
                dve_block(dve, NBLK, ctx_tiles, 1, CTX)

        def pe_block(pe, b, tiles, first):
            for r in range(tiles):
                pe.wait_ge(s_xr, b * R + (r + 1))
                for k in range(KD):
                    if r == 0 and not first:
                        pe.wait_ge(s_h, (b - 1) * KD + (k + 1))
                    t = nc.tensor.transpose(ps[:, k, r * P:(r + 1) * P], xt[:, r, k * P:(k + 1) * P], net.ident[:])
                    if r == tiles - 1:
                        t.then_inc(s_tr, 1)
                    if k == KD - 1 and r < tiles - 1:
                        t.then_inc(s_tile, 1)

        @block.tensor
        def _(pe):
            pe_block(pe, 0, R, True)
            with pe.Fori(1, NBLK) as b:
                pe_block(pe, b, R, False)
            if ctx_tiles:
                pe_block(pe, NBLK, ctx_tiles, False)


def in_proj(nc, net, hhi, hlo):
    RAW = KQ + KKV + 1
    with nc.cleanup_on_exit(), ExitStack() as st:
        sb = lambda n, s, d=F32: st.enter_context(nc.sbuf_tensor("inp_" + n, s, d))
        wst = sb("w", [P, 2, D])
        whi, wlo = sb("whi", [P, 2, D], F32R), sb("wlo", [P, 2, D], F32R)
        ob = sb("ob", [P, 4, BLK])
        sig = sb("sig", [P, 2, BLK])
        ps = st.enter_context(nc.psum_tensor("inp_ps", [P, 8, BLK], F32))
        s_w = net.sems("inp_w_in", 2)
        s_st = net.sems("inp_stored", 4)
        s_whi, s_wlo, s_out, s_sig, s_free = (net.sem("inp_" + n) for n in ("whi", "wlo", "out", "sig", "free"))
        block = st.enter_context(nc.Block())

        raw = [(m, b * BLK, BLK if b < NBLK else CTX) for m in range(RAW) for b in range(NBLK + (m >= KQ))]
        NRAW = len(raw)
        first_of = [min(i for i, o in enumerate(raw) if o[0] == m) for m in range(RAW)] + [NRAW]

        @block.sync
        def _(sp):
            for m in range(2):
                sp.dma_start(wst[:, m], net.w_in[m]).then_inc(s_w[m], 16)
            for o, (m, col, width) in enumerate(raw):
                if o == first_of[m]:
                    sp.wait_ge(s_wlo, m + 1)
                    sp.dma_start(wst[:, m % 2], net.w_in[m + 2]).then_inc(s_w[m % 2], 16)
                sp.wait_ge(s_free, o + 1)
                sp.dma_start(net.raw[m, :, col:col + width], ob[:, o % 4, 0:width]).then_inc(s_st[o % 4], 16)

            def pair(i, last):
                for r in range(2):
                    if not last:
                        sp.wait_ge(s_wlo, i * 2 + (RAW + r + 1))
                        sp.dma_start(wst[:, r], net.w_in[bass.ds(i * 2 + (RAW + r + 2), 1)].rearrange(
                            "a p n -> p (a n)")).then_inc(s_w[r], 16)
                    for b in range(NBLK):
                        o = NRAW + 4 * r + b
                        sp.wait_ge(s_free, i * 8 + (o + 1))
                        sp.dma_start(net.gate0[bass.ds(i * 2 + r, 1), :, b * BLK:(b + 1) * BLK].rearrange(
                            "a p n -> p (a n)"), ob[:, o % 4]).then_inc(s_st[o % 4], 16)

            with sp.Fori(0, HEADS // 2 - 1) as i:
                pair(i, False)
            pair(HEADS // 2 - 1, True)
            for k in range(4):
                sp.wait_ge(s_st[k], 16 * len(range(k, NRAW + HEADS * NBLK, 4)))

        def w_high(act, i, m):
            r = m % 2
            act.wait_ge(s_w[r], i * 16 + 16 * (m // 2 + 1))
            if m >= 2:
                act.wait_ge(s_out, i * 8 + (first_of[m - 1] if m <= RAW else NRAW + 4 * (m - RAW - 1)))
            nc.scalar.activation(whi[:, r], wst[:, r], ACT.Copy).then_inc(s_whi, 1)

        def w_low(dve, i, m):
            dve.wait_ge(s_whi, i * 2 + (m + 1))
            nc.vector.tensor_tensor(wlo[:, m % 2], wst[:, m % 2], whi[:, m % 2].bitcast(F32),
                                    ALU.subtract).then_inc(s_wlo, 1)

        @block.tensor
        def _(pe):
            def product(r, i, o, col, width):
                if not isinstance(i, int) or o >= 8:
                    pe.wait_ge(s_free, i * 8 + (o - 7))
                for k in range(KD):
                    mm = split3(nc, ps[:, o % 8, 0:width], whi[:, r, k * P:(k + 1) * P], wlo[:, r, k * P:(k + 1) * P],
                                hhi[:, k, col:col + width], hlo[:, k, col:col + width], k == 0, k == KD - 1)
                mm.then_inc(s_out, 1)

            for o, (m, col, width) in enumerate(raw):
                if o == first_of[m]:
                    pe.wait_ge(s_wlo, m + 1)
                product(m % 2, 0, o, col, width)
            with pe.Fori(0, HEADS // 2) as i:
                for r in range(2):
                    pe.wait_ge(s_wlo, i * 2 + (RAW + r + 1))
                    for b in range(NBLK):
                        product(r, i, NRAW + 4 * r + b, b * BLK, BLK)

        @block.scalar
        def _(act):
            w_high(act, 0, 0)
            for o, (m, col, width) in enumerate(raw):
                if o == first_of[m]:
                    w_high(act, 0, m + 1)
                act.wait_ge(s_out, o + 1)
                if o >= 4:
                    act.wait_ge(s_st[o % 4], 16 * (o // 4))
                nc.scalar.activation(ob[:, o % 4, 0:width], ps[:, o % 8, 0:width], ACT.Copy).then_inc(s_free, 1)

            def pair(i, last):
                for r in range(2):
                    if not (last and r):
                        w_high(act, i, RAW + r + 1)
                    for b in range(NBLK):
                        o = NRAW + 4 * r + b
                        act.wait_ge(s_out, i * 8 + (o + 1))
                        act.wait_ge(s_free, i * 8 + (o - 1))
                        nc.scalar.activation(sig[:, b % 2], ps[:, o % 8], ACT.Sigmoid).then_inc(s_sig, 1)

            with act.Fori(0, HEADS // 2 - 1) as i:
                pair(i, False)
            pair(HEADS // 2 - 1, True)

        @block.vector
        def _(dve):
            for m in range(RAW + 1):
                w_low(dve, 0, m)

            def pair(i, last):
                for r in range(2):
                    if not (last and r):
                        w_low(dve, i, RAW + r + 1)
                    for b in range(NBLK):
                        o = NRAW + 4 * r + b
                        dve.wait_ge(s_sig, i * 8 + (4 * r + b + 1))
                        dve.wait_ge(s_st[o % 4], i * 32 + 16 * (o // 4))
                        nc.vector.tensor_tensor(ob[:, o % 4], ps[:, o % 8], sig[:, b % 2],
                                                ALU.mult).then_inc(s_free, 1)

            with dve.Fori(0, HEADS // 2 - 1) as i:
                pair(i, False)
            pair(HEADS // 2 - 1, True)


def latents(nc, net, kind):
    isq = kind == "q"
    tag = kind + "u_"
    KC = KQ if isq else KKV
    raw0 = 0 if isq else KQ
    NROPE = HEADS // 2 if isq else 1
    blocks = [(b, b * BLK, BLK) for b in range(NBLK)] + ([] if isq else [(NBLK, SEQ, CTX)])
    ncols = HEADS * (NOPE + ROPE) if isq else HEADS * (NOPE + VDIM)

    def outputs(width):
        if isq:
            return [("rope", t, 0) for t in range(NROPE)] + [("nope", h, 0) for h in range(HEADS)]
        return [("key", h, 0) for h in range(HEADS)] + [("val", t, n) for t in range(width // P) for n in range(2)]

    NO = len(outputs(BLK))
    NW = ncols // BLK
    with nc.cleanup_on_exit(), ExitStack() as st:
        sb = lambda n, s, d=F32: st.enter_context(nc.sbuf_tensor(tag + n, s, d))
        wst = sb("w", [P, 2, KC, BLK])
        whi, wlo = sb("whi", [P, KC, ncols], F32R), sb("wlo", [P, KC, ncols], F32R)
        gain = sb("gain", [P, KC])
        xin = sb("xin", [P, 2, KC, BLK])
        krin = sb("krin", [P, 2, BLK])
        cs = sb("cs", [P, 2, 2, BLK])
        sq = sb("sq", [P, KC, BLK])
        ssum = sb("ssum", [P, BLK])
        rs = sb("rs", [P, BLK])
        xn = sb("xn", [P, KC, BLK])
        xhi, xlo = sb("xhi", [P, 2, KC, BLK], F32R), sb("xlo", [P, 2, KC, BLK], F32R)
        rq = sb("rq", [P, 2, BLK])
        t1, t2 = sb("t1", [P, BLK]), sb("t2", [P, BLK])
        ob = sb("ob", [P, 4, BLK])
        rob = sb("rob", [P, 2, BLK])
        ps = st.enter_context(nc.psum_tensor(tag + "ps", [P, 8, BLK], F32))
        SUM, PERM = 6, 7
        s_w = net.sems(tag + "w_in", 2)
        s_x = net.sems(tag + "x_in", 2)
        s_st = net.sems(tag + "stored", 4)
        s_rst = net.sems(tag + "rstored", 2)
        (s_gain, s_whi, s_wlo, s_sq, s_sum, s_ones, s_xn, s_xhi, s_xlo, s_out, s_ev, s_rq, s_perm, s_rope,
         s_rt, s_chain) = (net.sem(tag + n) for n in ("gain", "whi", "wlo", "sq", "sum", "ones", "xn", "xhi", "xlo", "out",
                                                "ev", "rq", "perm", "rope", "rt", "chain"))
        NLOAD = 3 if isq else 4
        w_dram = net.w_uq if isq else net.w_ukv
        block = st.enter_context(nc.Block())

        @block.sync
        def _(sp):
            sp.dma_start(gain[:], net.g_q if isq else net.g_kv).then_inc(s_gain, 16)

            def load(b, col, width):
                r = b % 2
                if b >= 2:
                    sp.wait_ge(s_xn, KC * (b - 1))
                    sp.wait_ge(s_rope, NROPE * (b - 1))
                sp.dma_start(xin[:, r, :, 0:width],
                             net.raw[raw0:raw0 + KC, :, col:col + width].rearrange("k p n -> p k n")).then_inc(s_x[r], 16)
                for t in range(2):
                    sp.dma_start(cs[:, r, t, 0:width], net.rope_tab[t, :, col:col + width]).then_inc(s_x[r], 16)
                if not isq:
                    sp.dma_start(krin[:, r, 0:width], net.raw[KQ + KKV, :, col:col + width]).then_inc(s_x[r], 16)

            for blk in blocks[:1]:
                load(*blk)
            for n in range(NW):
                if n >= 2:
                    sp.wait_ge(s_wlo, n - 1)
                sp.dma_start(wst[:, n % 2], w_dram[:, :, n * BLK:(n + 1) * BLK]).then_inc(s_w[n % 2], 16)
            load(*blocks[1])
            e = u = 0
            for b, col, width in blocks:
                for j, (what, t, n) in enumerate(outputs(width)):
                    if j == (NROPE if isq else 3):
                        for _ in range(NROPE):
                            sp.wait_ge(s_rope, u + 1)
                            dst = net.qr[u % NROPE, :, col:col + width] if isq else net.kr[:, col:col + width]
                            sp.dma_start(dst, rob[:, u % 2, 0:width]).then_inc(s_rst[u % 2], 16)
                            u += 1
                        if b + 2 < len(blocks):
                            load(*blocks[b + 2])
                    if what == "rope":
                        continue
                    sp.wait_ge(s_ev, NO * b + j + 1)
                    if what == "val":
                        dst = net.v[col // P + t, :, n * BLK:(n + 1) * BLK]
                    else:
                        dst = (net.qn if isq else net.kn)[t, :, col:col + width]
                    wd = BLK if what == "val" else width
                    sp.dma_start(dst, ob[:, e % 4, 0:wd]).then_inc(s_st[e % 4], 16)
                    e += 1
            for k in range(4):
                sp.wait_ge(s_st[k], 16 * len(range(k, e, 4)))
            for k in range(2):
                sp.wait_ge(s_rst[k], 16 * len(range(k, u, 2)))

        @block.scalar
        def _(act):
            def square(b, width):
                act.wait_ge(s_x[b % 2], 16 * NLOAD * (b // 2 + 1))
                if b:
                    act.wait_ge(s_sum, b)
                nc.scalar.activation(sq[:, :, 0:width], xin[:, b % 2, :, 0:width], ACT.Square).then_inc(s_sq, 1)

            def root(b, width):
                act.wait_ge(s_ones, b + 1)
                if b:
                    act.wait_ge(s_xn, KC * b)
                root_mean(nc, net, rs[:, 0:width], ps[:, SUM, 0:width], KC * P).then_inc(s_rt, 1)

            def high(b, width):
                if b >= 2:
                    act.wait_ge(s_out, NO * (b - 1))
                for k in range(KC):
                    act.wait_ge(s_xn, KC * b + k + 1)
                    nc.scalar.activation(xhi[:, b % 2, k, 0:width], xn[:, k, 0:width], ACT.Copy).then_inc(s_xhi, 1)

            square(0, BLK)
            root(0, BLK)
            for n in range(NW):
                act.wait_ge(s_w[n % 2], 16 * (n // 2 + 1))
                nc.scalar.activation(whi[:, :, n * BLK:(n + 1) * BLK], wst[:, n % 2], ACT.Copy).then_inc(s_whi, 1)
                if n == 0:
                    high(0, BLK)
            for b, col, width in blocks:
                outs = outputs(width)
                more = b + 1 < len(blocks)
                if more:
                    square(b + 1, blocks[b + 1][2])
                for j, (what, t, n) in enumerate(outs):
                    o = NO * b + j
                    act.wait_ge(s_out, o + 1)
                    wd = width if what != "val" else BLK
                    if what == "rope":
                        u = NROPE * b + t
                        if u >= 2:
                            act.wait_ge(s_rope, u - 1)
                        nc.scalar.activation(rq[:, t % 2, 0:wd], ps[:, o % 4, 0:wd], ACT.Copy).then_inc(s_rq, 1)
                        act.wait_ge(s_rq, u + 1)
                        act.sem_inc(s_ev, 1)
                    else:
                        e = o - NROPE * (b + 1) if isq else o
                        if e >= 4:
                            act.wait_ge(s_st[e % 4], 16 * (e // 4))
                        nc.scalar.activation(ob[:, e % 4, 0:wd], ps[:, o % 4, 0:wd], ACT.Copy).then_inc(s_ev, 1)
                    if j == 3 and more:
                        root(b + 1, blocks[b + 1][2])
                    if j == 6 and more:
                        high(b + 1, blocks[b + 1][2])

        @block.vector
        def _(dve):
            link = Chain(dve, s_chain)

            def norm(b, width):
                dve.wait_ge(s_sq, b + 1)
                if KC == 3:
                    link(nc.vector.tensor_tensor(ssum[:, 0:width], sq[:, 0, 0:width], sq[:, 1, 0:width], ALU.add))
                    nc.vector.tensor_tensor(ssum[:, 0:width], ssum[:, 0:width], sq[:, 2, 0:width],
                                            ALU.add).then_inc(s_sum, 1)
                else:
                    nc.vector.tensor_tensor(ssum[:, 0:width], sq[:, 0, 0:width], sq[:, 1, 0:width],
                                            ALU.add).then_inc(s_sum, 1)

            def scale(b, width):
                dve.wait_ge(s_rt, b + 1)
                link(nc.vector.reciprocal(rs[:, 0:width], rs[:, 0:width]))
                for k in range(KC):
                    nc.vector.scalar_tensor_tensor(out=xn[:, k, 0:width], in0=xin[:, b % 2, k, 0:width],
                                                   scalar=gain[:, k:k + 1], in1=rs[:, 0:width],
                                                   op0=ALU.mult, op1=ALU.mult).then_inc(s_xn, 1)
                for k in range(KC):
                    dve.wait_ge(s_xhi, KC * b + k + 1)
                    nc.vector.tensor_tensor(xlo[:, b % 2, k, 0:width], xn[:, k, 0:width],
                                            xhi[:, b % 2, k, 0:width].bitcast(F32), ALU.subtract).then_inc(s_xlo, 1)

            def rotate(b, t, width):
                u = NROPE * b + t
                src = rq[:, t % 2] if isq else krin[:, b % 2]
                dve.wait_ge(s_perm, u + 1)
                if u >= 2:
                    dve.wait_ge(s_rst[u % 2], 16 * (u // 2))
                nc.vector.tensor_tensor(t1[:, 0:width], src[:, 0:width], cs[:, b % 2, 0, 0:width], ALU.mult)
                link(nc.vector.tensor_tensor(t2[:, 0:width], ps[:, PERM, 0:width], cs[:, b % 2, 1, 0:width], ALU.mult))
                nc.vector.tensor_tensor(rob[:, u % 2, 0:width], t1[:, 0:width], t2[:, 0:width],
                                        ALU.add).then_inc(s_rope, 1)

            dve.wait_ge(s_gain, 16)
            norm(0, BLK)
            scale_done = False
            for n in range(NW):
                dve.wait_ge(s_whi, n + 1)
                nc.vector.tensor_tensor(wlo[:, :, n * BLK:(n + 1) * BLK], wst[:, n % 2],
                                        whi[:, :, n * BLK:(n + 1) * BLK].bitcast(F32), ALU.subtract).then_inc(s_wlo, 1)
                if n == 0:
                    scale(0, BLK)
            for b, col, width in blocks:
                more = b + 1 < len(blocks)
                if more:
                    norm(b + 1, blocks[b + 1][2])
                for t in range(NROPE):
                    rotate(b, t, width)
                if more:
                    scale(b + 1, blocks[b + 1][2])

        @block.tensor
        def _(pe):
            def column_sum(b, width):
                pe.wait_ge(s_sum, b + 1)
                nc.tensor.matmul(ps[:, SUM, 0:width], net.ones[:], ssum[:, 0:width], start=True,
                                 stop=True).then_inc(s_ones, 1)

            def permute(b, t, width):
                u = NROPE * b + t
                src = rq[:, t % 2] if isq else krin[:, b % 2]
                if isq:
                    pe.wait_ge(s_rq, u + 1)
                else:
                    pe.wait_ge(s_x[b % 2], 16 * NLOAD * (b // 2 + 1))
                if u:
                    pe.wait_ge(s_rope, u)
                nc.tensor.matmul(ps[:, PERM, 0:width], net.perm[:], src[:, 0:width], start=True,
                                 stop=True).then_inc(s_perm, 1)

            column_sum(0, BLK)
            for b, col, width in blocks:
                r = b % 2
                pe.wait_ge(s_xlo, KC * (b + 1))
                for j, (what, t, n) in enumerate(outputs(width)):
                    o = NO * b + j
                    if o >= 4:
                        pe.wait_ge(s_ev, o - 3)
                    if b == 0:
                        cols = {"rope": t * P, "nope": NROPE * P + t * P, "key": t * P, "val": HEADS * P + n * BLK}[what]
                        pe.wait_ge(s_wlo, cols // BLK + 1)
                    for k in range(KC):
                        first, last = k == 0, k == KC - 1
                        if what == "val":
                            wcol = slice(HEADS * P + n * BLK, HEADS * P + (n + 1) * BLK)
                            tok = slice(t * P, (t + 1) * P)
                            mm = split3(nc, ps[:, o % 4], xhi[:, r, k, tok], xlo[:, r, k, tok],
                                        whi[:, k, wcol], wlo[:, k, wcol], first, last)
                        else:
                            w0 = t * P + (NROPE * P if what == "nope" else 0)
                            mm = split3(nc, ps[:, o % 4, 0:width], whi[:, k, w0:w0 + P], wlo[:, k, w0:w0 + P],
                                        xhi[:, r, k, 0:width], xlo[:, r, k, 0:width], first, last)
                    mm.then_inc(s_out, 1)
                    if j == 1 and b + 1 < len(blocks):
                        column_sum(b + 1, blocks[b + 1][2])
                    if 1 <= j <= NROPE:
                        permute(b, j - 1, width)


def attention(nc, net):
    QT = BLK // P
    NBH = SEQ // BLK
    slots = list(range(NKT // 2)) + ["den"] + list(range(NKT // 2, NKT))
    cuts = [0, 5, 10, 15, SLOTS]
    with nc.cleanup_on_exit(), ExitStack() as st:
        sb = lambda n, s, d=F32: st.enter_context(nc.sbuf_tensor("at_" + n, s, d))
        prob = sb("prob", [P, 2, QT, TOK])
        kst = sb("kst", [P, TOK])
        vst = sb("vst", [P, NKT, VDIM])
        khi, klo = sb("khi", [P, TOK], F32R), sb("klo", [P, TOK], F32R)
        vhi, vlo = sb("vhi", [P, NKT, VDIM], F32R), sb("vlo", [P, NKT, VDIM], F32R)
        krhi, krlo = sb("krhi", [P, TOK], F32R), sb("krlo", [P, TOK], F32R)
        qst, qrst = sb("qst", [P, 2, BLK]), sb("qrst", [P, 2, BLK])
        qhi, qlo = sb("qhi", [P, 2, BLK], F32R), sb("qlo", [P, 2, BLK], F32R)
        qr = sb("qr", [P, 2, BLK], F32R)
        pthi, ptlo = sb("pthi", [P, 3, BLK], F32R), sb("ptlo", [P, 3, BLK], F32R)
        mx = sb("mx", [P, 2, 8])
        nmax = sb("nmax", [P, 2])
        lsum = sb("lsum", [P, 2, 8])
        rl = sb("rl", [P, 2])
        dg = sb("dg", [P, 2, BLK])
        den = sb("den", [P, BLK])
        gst = sb("gst", [P, 2, BLK])
        gden = sb("gden", [P, BLK])
        og = sb("og", [P, 2, BLK])
        S = st.enter_context(nc.psum_tensor("at_S", [P, NCHUNK, BLK], F32))
        T = st.enter_context(nc.psum_tensor("at_T", [P, 2, BLK], F32))
        O = st.enter_context(nc.psum_tensor("at_O", [P, BLK], F32))
        s_q = net.sems("at_q_in", 2)
        s_g = net.sems("at_g_in", 2)
        s_ogst = net.sems("at_og_stored", 2)
        (s_k, s_v, s_krin, s_krhi, s_kr, s_khi, s_klo, s_vhi, s_vlo, s_qhi, s_qlo, s_qk, s_mx, s_nmax, s_exp, s_rl, s_dg,
         s_tr, s_hi, s_lo, s_mm, s_gden, s_og, s_recip) = (net.sem("at_" + n) for n in (
             "k_in", "v_in", "kr_in", "krhi", "kr", "khi", "klo", "vhi", "vlo", "qhi", "qlo", "qk", "mx", "nmax", "exp",
             "rl", "dg", "tr", "hi", "lo", "mm", "gden", "og", "recip"))
        VC = 3
        KPV = NKT // VC
        block = st.enter_context(nc.Block())

        def index(h, j):
            return h * NBH + j

        def head1(t, h, *rest):
            return t[bass.ds(h, 1)] if not isinstance(h, int) else t[h:h + 1]

        def load_q(sp, h, j):
            h, j, r = h + j // NBH, j % NBH, j % 2
            cols = slice(j * BLK, (j + 1) * BLK)
            sp.dma_start(qst[:, r], head1(net.qn, h)[:, :, cols].rearrange("a p n -> p (a n)")).then_inc(s_q[r], 16)
            for half in range(2):
                sp.dma_start(qrst[half * ROPE:(half + 1) * ROPE, r],
                             head1(net.qr_heads, h)[:, :, cols].rearrange("a p n -> p (a n)")).then_inc(s_q[r], 16)

        def load_gate(sp, h, j):
            sp.dma_start(gst[:, j % 2], head1(net.gate0, h)[:, :, j * BLK:(j + 1) * BLK].rearrange("a p n -> p (a n)")
                         ).then_inc(s_g[j % 2], 16)

        def load_k(sp, h):
            sp.dma_start(kst[:], head1(net.kn, h).rearrange("a p n -> p (a n)")).then_inc(s_k, 16)

        def load_v(sp, h):
            if isinstance(h, int):
                src = net.v[:, :, h * VDIM:(h + 1) * VDIM]
            else:
                src = net.v[:, :, bass.ds(h * VDIM, VDIM)]
            sp.dma_start(vst[:], src.rearrange("t p d -> p t d")).then_inc(s_v, 16)

        @block.sync
        def _(sp):
            load_q(sp, 0, 0)
            load_k(sp, 0)
            sp.dma_start(prob[:, 1, 0], net.kr).then_inc(s_krin, 16)
            load_v(sp, 0)
            load_q(sp, 0, 1)
            load_gate(sp, 0, 0)
            sp.wait_ge(s_qlo, 1)
            load_q(sp, 0, 2)

            def phase(h, j, last):
                b = index(h, j)
                if not last and j == 0:
                    sp.wait_ge(s_klo, h * NCHUNK + NCHUNK)
                    load_k(sp, h + 1)
                if not last and j == 1:
                    sp.wait_ge(s_vlo, h * VC + VC)
                    load_v(sp, h + 1)
                if not last or j + 1 < NBH:
                    if not isinstance(h, int) or h or j:
                        sp.wait_ge(s_gden, b)
                    nh, nj = (h, j + 1) if j + 1 < NBH else (h + 1, 0)
                    load_gate(sp, nh, nj)
                if not last or j + 3 < NBH:
                    sp.wait_ge(s_qlo, b + 2)
                    load_q(sp, h, j + 3)

            for j in range(NBH):
                phase(0, j, False)
            with sp.Fori(1, HEADS - 1) as h:
                for j in range(NBH):
                    phase(h, j, False)
            for j in range(NBH):
                phase(HEADS - 1, j, True)

        @block.tensor
        def _(pe):
            def scores(h, j, i, c):
                b = index(h, j)
                t = b * QT + i
                if i == 0 and c == 0:
                    pe.wait_ge(s_qlo, b + 1)
                if j == 0 and i == 0:
                    pe.wait_ge(s_klo, h * NCHUNK + (c + 1))
                if not (isinstance(t, int) and t == 0):
                    pe.wait_ge(s_exp, (t - 1) * NCHUNK + (c + 1))
                r, q, k = j % 2, slice(i * P, (i + 1) * P), chunk(c)
                out = S[:, c, 0:k.stop - k.start]
                nc.tensor.matmul(out, qhi[:, r, q], khi[:, k], start=True, stop=False)
                nc.tensor.matmul(out, qhi[:, r, q], klo[:, k], start=False, stop=False)
                nc.tensor.matmul(out, qlo[:, r, q], khi[:, k], start=False, stop=False)
                nc.tensor.matmul(out, qr[:, r, q], krhi[:, k], start=False, stop=False)
                nc.tensor.matmul(out, qr[:, r, q], krlo[:, k], start=False, stop=True).then_inc(s_qk, 1)

            def transposes(h, j, n):
                b = index(h, j)
                m = n + SLOTS * j
                if not (isinstance(h, int) and h == 0 and m < 2):
                    prev = (n - 2) % SLOTS
                    if slots[prev] == "den":
                        pe.wait_ge(s_hi, h * (SLOTS * NBH) + (m - 1))
                    else:
                        before = sum(1 for x in range(n - 1 if n >= 2 else SLOTS + n - 1) if slots[x] != "den")
                        pe.wait_ge(s_lo, (b if n >= 2 else b - 1) * NKT + before)
                out = T[:, m % 2]
                kt = slots[n]
                if kt == "den":
                    pe.wait_ge(s_dg, b * QT + QT)
                    for i in range(QT):
                        mm = nc.tensor.matmul(out[:, i * P:(i + 1) * P], net.ones[:], dg[:, j % 2, i * P:(i + 1) * P],
                                              start=True, stop=True)
                else:
                    if n == 0:
                        pe.wait_ge(s_exp, b * (QT * NCHUNK) + QT * NCHUNK)
                    for i in range(QT):
                        mm = nc.tensor.transpose(out[:, i * P:(i + 1) * P], prob[:, j % 2, i, kt * P:(kt + 1) * P],
                                                 net.ident[:])
                mm.then_inc(s_tr, 1)

            def values(h, j, n):
                kt = slots[n]
                if kt == "den":
                    return
                b = index(h, j)
                if j == 0 and kt % KPV == 0:
                    pe.wait_ge(s_vlo, h * VC + (kt // KPV + 1))
                if kt == 0 and not (isinstance(b, int) and b == 0):
                    pe.wait_ge(s_og, b)
                pe.wait_ge(s_lo, b * NKT + (kt + 1))
                r = kt % 3
                split3(nc, O[:], vhi[:, kt], vlo[:, kt], pthi[:, r], ptlo[:, r], kt == 0,
                       kt == NKT - 1).then_inc(s_mm, 1)

            def phase(h, j, with_scores=True):
                nh, nj = (h, j + 1) if j + 1 < NBH else (h + 1, 0)
                for i in range(QT):
                    ns = list(range(cuts[i], cuts[i + 1]))
                    for c in range(NCHUNK):
                        if with_scores:
                            scores(nh, nj, i, c)
                        if c < 3:
                            step(h, j, ns[c])
                    for n in ns[3:]:
                        step(h, j, n)
                for n in (SLOTS - 2, SLOTS - 1):
                    values(h, j, n)

            def step(h, j, n):
                transposes(h, j, n)
                if n >= 2:
                    values(h, j, n - 2)

            pe.wait_ge(s_kr, 1)
            for i in range(QT):
                for c in range(NCHUNK):
                    scores(0, 0, i, c)
            for j in range(NBH):
                phase(0, j)
            with pe.Fori(1, HEADS - 1) as h:
                for j in range(NBH):
                    phase(h, j)
            for j in range(NBH):
                phase(HEADS - 1, j, j + 1 < NBH)

        @block.scalar
        def _(act):
            def k_high(h):
                if isinstance(h, int):
                    act.wait_ge(s_k, 16 * (h + 1))
                else:
                    act.wait_ge(s_k, h * 16 + 16)
                if not (isinstance(h, int) and h == 0):
                    act.wait_ge(s_qk, h * (NBH * QT * NCHUNK))
                for c in range(NCHUNK):
                    nc.scalar.activation(khi[:, chunk(c)], kst[:, chunk(c)], ACT.Copy).then_inc(s_khi, 1)

            def v_high(h):
                act.wait_ge(s_v, h * 16 + 16)
                if not (isinstance(h, int) and h == 0):
                    act.wait_ge(s_mm, h * (NBH * NKT))
                for c in range(VC):
                    nc.scalar.activation(vhi[:, c * KPV:(c + 1) * KPV], vst[:, c * KPV:(c + 1) * KPV],
                                         ACT.Copy).then_inc(s_vhi, 1)

            def q_high(h, j):
                h, j = h + j // NBH, j % NBH
                b, r = index(h, j), j % 2
                act.wait_ge(s_q[r], h * (48 * NBH // 2) + 48 * (j // 2 + 1))
                if not (isinstance(b, int) and b < 2):
                    act.wait_ge(s_qk, (b - 1) * (QT * NCHUNK))
                nc.scalar.activation(qhi[:, r], qst[:, r], ACT.Copy).then_inc(s_qhi, 1)
                nc.scalar.activation(qr[:, r], qrst[:, r], ACT.Copy).then_inc(s_qhi, 1)

            def exponential(h, j, i, c):
                b = index(h, j)
                t = b * QT + i
                if c == 0:
                    act.wait_ge(s_nmax, t + 1)
                    if not (isinstance(t, int) and t < 2):
                        act.wait_ge(s_rl, t - 1)
                    if i == 0 and not (isinstance(b, int) and b < 2):
                        act.wait_ge(s_tr, (b - 1) * SLOTS)
                k = chunk(c)
                nc.scalar.activation(prob[:, j % 2, i, k], S[:, c, 0:k.stop - k.start], ACT.Exp, scale=SCALE,
                                     bias=nmax[:, i % 2:i % 2 + 1],
                                     accum_out=lsum[:, i % 2, c:c + 1]).then_inc(s_exp, 1)

            def high(h, j, n):
                b = index(h, j)
                act.wait_ge(s_tr, h * (SLOTS * NBH) + (n + SLOTS * j + 1))
                kt = slots[n]
                if kt == "den":
                    if not (isinstance(b, int) and b == 0):
                        act.wait_ge(s_gden, b)
                    dst = den[:]
                else:
                    if not (isinstance(b, int) and b == 0 and kt < 3):
                        act.wait_ge(s_mm, b * NKT + (kt - 2))
                    dst = pthi[:, kt % 3]
                nc.scalar.activation(dst, T[:, (n + SLOTS * j) % 2], ACT.Copy).then_inc(s_hi, 1)

            def store_output(h, j):
                act.wait_ge(s_og, index(h, j) + 1)
                act.dma_start(head1(net.og, h)[:, :, j * BLK:(j + 1) * BLK].rearrange("a p n -> p (a n)"),
                              og[:, j % 2]).then_inc(s_ogst[j % 2], 16)

            def phase(h, j, last=False):
                nh, nj = (h, j + 1) if j + 1 < NBH else (h + 1, 0)
                with_scores = not last or j + 1 < NBH
                if j == NBH - 1 and with_scores:
                    k_high(h + 1)
                for i in range(QT):
                    ns = list(range(cuts[i], cuts[i + 1]))
                    for n in ns[:3]:
                        high(h, j, n)
                    if i == 1 and (not last or j + 2 < NBH):
                        q_high(h, j + 2)
                    if i == 1 and not (isinstance(h, int) and h == 0 and j == 0):
                        store_output(*((h, j - 1) if j else (h - 1, NBH - 1)))
                    if with_scores:
                        exponential(nh, nj, i, 0)
                    high(h, j, ns[3])
                    if with_scores:
                        exponential(nh, nj, i, 1)
                        exponential(nh, nj, i, 2)
                    if len(ns) > 4:
                        high(h, j, ns[4])
                    if with_scores:
                        exponential(nh, nj, i, 3)
                        exponential(nh, nj, i, 4)
                if j == NBH - 1 and not last:
                    v_high(h + 1)

            act.wait_ge(s_krin, 16)
            nc.scalar.activation(krhi[:], prob[:, 1, 0], ACT.Copy).then_inc(s_krhi, 1)
            q_high(0, 0)
            k_high(0)
            for i in range(QT):
                for c in range(NCHUNK):
                    exponential(0, 0, i, c)
                if i == 1:
                    q_high(0, 1)
            v_high(0)
            for j in range(NBH):
                phase(0, j)
            with act.Fori(1, HEADS - 1) as h:
                for j in range(NBH):
                    phase(h, j)
            for j in range(NBH):
                phase(HEADS - 1, j, True)
            store_output(HEADS - 1, NBH - 1)
            for k in range(2):
                act.wait_ge(s_ogst[k], 16 * HEADS * NBH // 2)

        @block.vector
        def _(dve):
            def k_low(h):
                for c in range(NCHUNK):
                    dve.wait_ge(s_khi, h * NCHUNK + (c + 1))
                    nc.vector.tensor_tensor(klo[:, chunk(c)], kst[:, chunk(c)], khi[:, chunk(c)].bitcast(F32),
                                            ALU.subtract).then_inc(s_klo, 1)

            def v_low(h):
                for c in range(VC):
                    dve.wait_ge(s_vhi, h * VC + (c + 1))
                    v = slice(c * KPV, (c + 1) * KPV)
                    nc.vector.tensor_tensor(vlo[:, v], vst[:, v], vhi[:, v].bitcast(F32),
                                            ALU.subtract).then_inc(s_vlo, 1)

            def q_low(h, j):
                h, j = h + j // NBH, j % NBH
                b, r = index(h, j), j % 2
                dve.wait_ge(s_qhi, b * 2 + 2)
                nc.vector.tensor_tensor(qlo[:, r], qst[:, r], qhi[:, r].bitcast(F32), ALU.subtract)
                nc.vector.tensor_tensor(qr[ROPE:P, r], qrst[ROPE:P, r], qr[ROPE:P, r].bitcast(F32),
                                        ALU.subtract).then_inc(s_qlo, 1)

            def maximum(h, j, i, c):
                t = index(h, j) * QT + i
                dve.wait_ge(s_qk, t * NCHUNK + (c + 1))
                k = chunk(c)
                nc.vector.tensor_reduce(mx[:, i % 2, c:c + 1], S[:, c, 0:k.stop - k.start], AXX,
                                        ALU.max).then_inc(s_mx, 1)

            def negated(h, j, i):
                t = index(h, j) * QT + i
                dve.wait_ge(s_mx, t * (NCHUNK + 1) + NCHUNK)
                nc.vector.tensor_reduce(mx[:, i % 2, 7:8], mx[:, i % 2, 0:NCHUNK], AXX, ALU.max).then_inc(s_mx, 1)
                dve.wait_ge(s_mx, (t + 1) * (NCHUNK + 1))
                if not (isinstance(t, int) and t < 2):
                    dve.wait_ge(s_exp, (t - 1) * NCHUNK)
                nc.vector.tensor_scalar(nmax[:, i % 2:i % 2 + 1], mx[:, i % 2, 7:8], -SCALE, None,
                                        ALU.mult).then_inc(s_nmax, 1)

            def denominator(h, j, i):
                b = index(h, j)
                t = b * QT + i
                dve.wait_ge(s_exp, (t + 1) * NCHUNK)
                nc.vector.tensor_reduce(lsum[:, i % 2, 7:8], lsum[:, i % 2, 0:NCHUNK], AXX, ALU.add).then_inc(s_rl, 1)
                dve.wait_ge(s_rl, t + 1)
                nc.vector.reciprocal(rl[:, i % 2:i % 2 + 1], lsum[:, i % 2, 7:8]).then_inc(s_recip, 1)
                dve.wait_ge(s_recip, t + 1)
                if i == 0 and not (isinstance(b, int) and b < 2):
                    dve.wait_ge(s_tr, (b - 1) * SLOTS)
                nc.vector.tensor_scalar(dg[:, j % 2, i * P:(i + 1) * P], net.ident[:], rl[:, i % 2:i % 2 + 1], None,
                                        ALU.mult).then_inc(s_dg, 1)

            def low(h, j, n):
                kt = slots[n]
                if kt == "den":
                    return
                dve.wait_ge(s_hi, h * (SLOTS * NBH) + (n + SLOTS * j + 1))
                nc.vector.tensor_tensor(ptlo[:, kt % 3], T[:, (n + SLOTS * j) % 2], pthi[:, kt % 3].bitcast(F32),
                                        ALU.subtract).then_inc(s_lo, 1)

            def output(h, j):
                b = index(h, j)
                dve.wait_ge(s_mm, b * NKT + NKT)
                dve.wait_ge(s_gden, b + 1)
                if not (isinstance(h, int) and h == 0 and j < 2):
                    dve.wait_ge(s_ogst[j % 2], h * (16 * NBH // 2) + 16 * (j // 2))
                nc.vector.tensor_tensor(og[:, j % 2], O[:], gden[:], ALU.mult).then_inc(s_og, 1)

            def phase(h, j, last=False):
                nh, nj = (h, j + 1) if j + 1 < NBH else (h + 1, 0)
                with_scores = not last or j + 1 < NBH
                if j == NBH - 1 and with_scores:
                    k_low(h + 1)
                for i in range(QT):
                    ns = list(range(cuts[i], cuts[i + 1]))
                    for c in range(NCHUNK):
                        if with_scores:
                            maximum(nh, nj, i, c)
                        if c < 3:
                            low(h, j, ns[c])
                        if c == 1:
                            if i:
                                if with_scores:
                                    denominator(nh, nj, i - 1)
                            else:
                                denominator(h, j, QT - 1)
                    if with_scores:
                        negated(nh, nj, i)
                    if i == 1 and (not last or j + 2 < NBH):
                        q_low(h, j + 2)
                    for n in ns[3:]:
                        low(h, j, n)
                output(h, j)
                if j == NBH - 1 and not last:
                    v_low(h + 1)

            dve.wait_ge(s_krhi, 1)
            nc.vector.tensor_tensor(krlo[:], prob[:, 1, 0], krhi[:].bitcast(F32), ALU.subtract).then_inc(s_kr, 1)
            q_low(0, 0)
            k_low(0)
            for i in range(QT):
                for c in range(NCHUNK):
                    maximum(0, 0, i, c)
                negated(0, 0, i)
                if i:
                    denominator(0, 0, i - 1)
                if i == 1:
                    q_low(0, 1)
            v_low(0)
            for j in range(NBH):
                phase(0, j)
            with dve.Fori(1, HEADS - 1) as h:
                for j in range(NBH):
                    phase(h, j)
            for j in range(NBH):
                phase(HEADS - 1, j, True)

        @block.gpsimd
        def _(pool):
            def gate(h, j):
                b = index(h, j)
                pool.wait_ge(s_hi, h * (SLOTS * NBH) + (slots.index("den") + 1 + SLOTS * j))
                pool.wait_ge(s_g[j % 2], h * (16 * NBH // 2) + 16 * (j // 2 + 1))
                if not (isinstance(b, int) and b == 0):
                    pool.wait_ge(s_og, b)
                nc.gpsimd.tensor_tensor(gden[:], den[:], gst[:, j % 2], ALU.mult).then_inc(s_gden, 1)

            for j in range(NBH):
                gate(0, j)
            with pool.Fori(1, HEADS) as h:
                for j in range(NBH):
                    gate(h, j)




def attn_out(nc, net):
    W = 256
    NB = SEQ // W
    TB = W // P
    with nc.cleanup_on_exit(), ExitStack() as st:
        sb = lambda n, s, d=F32: st.enter_context(nc.sbuf_tensor("ao_" + n, s, d))
        wst = sb("w", [P, 2, D])
        whi, wlo = sb("whi", [P, KD, D], F32R), sb("wlo", [P, KD, D], F32R)
        oin = sb("oin", [P, 2, KD, W])
        ohi, olo = sb("ohi", [P, 2, KD, W], F32R), sb("olo", [P, 2, KD, W], F32R)
        xt = sb("x", [P, 2 * TB, D])
        gp = sb("gp", [P, D])
        tmp = sb("tmp", [P, D])
        junk = sb("junk", [P, D])
        ob = sb("ob", [P, 2, D])
        ss, rs = sb("ss", [P, 4]), sb("rs", [P, 4])
        ps = st.enter_context(nc.psum_tensor("ao_ps", [P, 4, D], F32))
        s_w, s_o = net.sems("ao_w_in", 2), net.sems("ao_o_in", 2)
        s_x, s_st = net.sems("ao_x_in", 2 * TB), net.sems("ao_stored", 2)
        (s_gp, s_whi, s_wlo, s_ohi, s_olo, s_y, s_ss, s_rt, s_rs, s_tmp, s_x1) = (
            net.sem("ao_" + n) for n in ("gp", "whi", "wlo", "ohi", "olo", "y", "ss", "rt", "rs", "tmp", "x1"))
        block = st.enter_context(nc.Block())

        def nxt(i, r):
            return (i, 1) if r == 0 else (i + 1, 0)

        def loop(eng, body):
            body(0, False)
            with eng.Fori(1, NB // 2 - 1) as i:
                body(i, False)
            body(NB // 2 - 1, True)

        def load_o(sp, i, r):
            sp.dma_start(oin[:, r], net.og[:, :, bass.ds(i * (2 * W) + r * W, W)].rearrange("k p n -> p k n")
                         ).then_inc(s_o[r], 16)

        def load_x(sp, i, s):
            sp.dma_start(xt[:, s], net.x[bass.ds(i * (2 * W) + s * P, P), :]).then_inc(s_x[s], 16)

        @block.sync
        def _(sp):
            load_o(sp, 0, 0)
            for k in range(KD):
                if k >= 2:
                    sp.wait_ge(s_wlo, k - 1)
                sp.dma_start(wst[:, k % 2], net.w_o0[:, k]).then_inc(s_w[k % 2], 16)
            load_o(sp, 0, 1)
            sp.dma_start(gp[:], net.gp_flat[0:1, :].to_broadcast([P, D])).then_inc(s_gp, 16)
            for s in range(2 * TB):
                load_x(sp, 0, s)

            def body(i, last):
                for r in range(2):
                    if not last:
                        sp.wait_ge(s_olo, i * 2 + (r + 1))
                        load_o(sp, i + 1, r)
                    for s in range(TB * r, TB * r + TB):
                        sp.wait_ge(s_x1, i * 4 + (s + 1))
                        sp.dma_start(net.x1[bass.ds(i * (2 * W) + s * P, P), :], ob[:, s % 2]
                                     ).then_inc(s_st[s % 2], 16)
                        if not last:
                            load_x(sp, i + 1, s)

            loop(sp, body)
            for k in range(2):
                sp.wait_ge(s_st[k], 16 * SEQ // P // 2)

        def o_high(act, i, r):
            act.wait_ge(s_o[r], i * 16 + 16)
            if not isinstance(i, int) or i:
                act.wait_ge(s_y, i * 4 + TB * (r - 1))
            nc.scalar.activation(ohi[:, r], oin[:, r], ACT.Copy).then_inc(s_ohi, 1)

        @block.scalar
        def _(act):
            o_high(act, 0, 0)
            for k in range(KD):
                act.wait_ge(s_w[k % 2], 16 * (k // 2 + 1))
                nc.scalar.activation(whi[:, k], wst[:, k % 2], ACT.Copy).then_inc(s_whi, 1)

            def body(i, last):
                for r in range(2):
                    if not (last and r):
                        o_high(act, *nxt(i, r))
                    for s in range(TB * r, TB * r + TB):
                        act.wait_ge(s_y, i * 4 + (s + 1))
                        if not isinstance(i, int) or i:
                            act.wait_ge(s_tmp, i * 4 + (s - 3))
                        nc.scalar.activation(junk[:], ps[:, s], ACT.Square, accum_out=ss[:, s:s + 1]).then_inc(s_ss, 1)
                        act.wait_ge(s_ss, i * 4 + (s + 1))
                        root_mean(nc, net, rs[:, s:s + 1], ss[:, s:s + 1], D).then_inc(s_rt, 1)

            loop(act, body)

        @block.vector
        def _(dve):
            def o_low(i, r):
                dve.wait_ge(s_ohi, i * 2 + (r + 1))
                nc.vector.tensor_tensor(olo[:, r], oin[:, r], ohi[:, r].bitcast(F32), ALU.subtract).then_inc(s_olo, 1)

            o_low(0, 0)
            for k in range(KD):
                dve.wait_ge(s_whi, k + 1)
                nc.vector.tensor_tensor(wlo[:, k], wst[:, k % 2], whi[:, k].bitcast(F32),
                                        ALU.subtract).then_inc(s_wlo, 1)
            dve.wait_ge(s_gp, 16)

            def body(i, last):
                for r in range(2):
                    if not (last and r):
                        o_low(*nxt(i, r))
                    for s in range(TB * r, TB * r + TB):
                        dve.wait_ge(s_rt, i * 4 + (s + 1))
                        nc.vector.reciprocal(rs[:, s:s + 1], rs[:, s:s + 1]).then_inc(s_rs, 1)
                        dve.wait_ge(s_rs, i * 4 + (s + 1))
                        nc.vector.scalar_tensor_tensor(out=tmp[:], in0=ps[:, s], scalar=rs[:, s:s + 1], in1=gp[:],
                                                       op0=ALU.mult, op1=ALU.mult).then_inc(s_tmp, 1)
                        dve.wait_ge(s_tmp, i * 4 + (s + 1))
                        dve.wait_ge(s_x[s], i * 16 + 16)
                        if s >= 2 or not isinstance(i, int) or i:
                            dve.wait_ge(s_st[s % 2], i * 32 + 16 * (s // 2))
                        nc.vector.tensor_tensor(ob[:, s % 2], tmp[:], xt[:, s], ALU.add).then_inc(s_x1, 1)

            loop(dve, body)

        @block.tensor
        def _(pe):
            def body(i, last):
                for r in range(2):
                    pe.wait_ge(s_olo, i * 2 + (r + 1))
                    for s in range(TB * r, TB * r + TB):
                        if not isinstance(i, int) or i:
                            pe.wait_ge(s_tmp, i * 4 + (s - 3))
                        tok = slice((s % TB) * P, (s % TB + 1) * P)
                        for n in range(2):
                            c = slice(n * BLK, (n + 1) * BLK)
                            for k in range(KD):
                                if isinstance(i, int) and i == 0 and s == 0 and n == 0:
                                    pe.wait_ge(s_wlo, k + 1)
                                mm = split3(nc, ps[:, s, c], ohi[:, r, k, tok], olo[:, r, k, tok],
                                            whi[:, k, c], wlo[:, k, c], k == 0, k == KD - 1)
                        mm.then_inc(s_y, 1)

            loop(pe, body)


def conv_in(nc, net, hhi, hlo):
    GROUPS = D // P
    CH = P // CCH
    with nc.cleanup_on_exit(), ExitStack() as st:
        sb = lambda n, s, d=F32: st.enter_context(nc.sbuf_tensor("ci_" + n, s, d))
        wst = sb("w", [P, 3, D])
        whi, wlo = sb("whi", [P, 3, D], F32R), sb("wlo", [P, 3, D], F32R)
        sig = sb("sig", [P, 2, BLK])
        ub, gb = sb("ub", [P, 2, PHASES, BLK // PHASES]), sb("gb", [P, 2, PHASES, BLK // PHASES])
        raw = sb("raw", [P, 4, NCOL])
        HALO = OFFS // 2
        uhi, ulo = (sb(n, [P, 2, NCOL + 2 * HALO], F32R) for n in ("uhi", "ulo"))
        taps = sb("taps", [P, CH, OFFS * PHASES])
        thi, tlo = sb("thi", [P, CH, OFFS * PHASES], F32R), sb("tlo", [P, CH, OFFS * PHASES])
        bhi, blo = (sb(n, [P, 2, OFFS, CCH, PHASES], F32R) for n in ("bhi", "blo"))
        mask, bdw = sb("mask", [P, CCH]), sb("bdw", [P, GROUPS * CH])
        zb = sb("zb", [P, 2, NCOL])
        ps = st.enter_context(nc.psum_tensor("ci_ps", [P, 8, BLK], F32))
        s_w = net.sems("ci_w_in", 3)
        s_ust, s_gst, s_zst = net.sems("ci_u_stored", 2), net.sems("ci_g_stored", 2), net.sems("ci_z_stored", 2)
        s_raw = net.sems("ci_raw_in", 4)
        (s_const, s_pad, s_taps, s_whi, s_wlo, s_ab, s_g, s_sig, s_mul, s_thi, s_tlo, s_uhi, s_ulo, s_bhi, s_blo, s_cv,
         s_z) = (net.sem("ci_" + n) for n in (
             "const", "pad", "taps", "whi", "wlo", "ab", "g", "sig", "mul", "thi", "tlo", "uhi", "ulo", "bhi", "blo",
             "cv", "z"))
        block = st.enter_context(nc.Block())
        B, A, G = range(3)

        def banded(t):
            return (t.rearrange("p (j f) -> p j f", j=OFFS).unsqueeze(2).to_broadcast([P, OFFS, CCH, PHASES]),
                    mask[:].unsqueeze(1).unsqueeze(3).to_broadcast([P, OFFS, CCH, PHASES]))

        def loop(eng, body):
            body(0, True, False)
            with eng.Fori(1, GROUPS - 1) as g:
                body(g, False, False)
            body(GROUPS - 1, False, True)

        def load_w(sp, g, s):
            sp.dma_start(wst[:, s], net.cv_w_in[bass.ds(g * 3 + s, 1)].rearrange("a p n -> p (a n)")
                         ).then_inc(s_w[s], 16)

        def columns(dram, g, b):
            return dram[bass.ds(g, 1), :, :, b * (BLK // PHASES):(b + 1) * (BLK // PHASES)].rearrange(
                "a c s n -> c (a s) n")

        def load_u(sp, g, q):
            sp.dma_start(raw[:, q % 4], net.u_chunks[bass.ds(g * CH + q, 1)].rearrange("a p n -> p (a n)")
                         ).then_inc(s_raw[q % 4], 16)

        @block.sync
        def _(sp):
            for s in range(3):
                load_w(sp, 0, s)
            sp.dma_start(mask[:], net.mask_in).then_inc(s_const, 16)
            sp.dma_start(bdw[:], net.b_dw).then_inc(s_const, 16)

            def body(g, first, last):
                if not first:
                    sp.wait_ge(s_tlo, g)
                sp.dma_start(taps[:], net.taps[bass.ds(g, 1)].rearrange("a p q t -> p (a q) t")).then_inc(s_taps, 16)
                if not last:
                    for s in (B, A, G):
                        sp.wait_ge(s_wlo, g * 3 + (s + 1))
                        load_w(sp, g + 1, s)
                for b in range(NBLK):
                    sp.wait_ge(s_mul, g * 8 + (b + 1))
                    sp.dma_start(columns(net.u_phases, g, b), ub[:, b % 2]).then_inc(s_ust[b % 2], 16)
                if not first:
                    sp.wait_ge(s_ulo, g * CH)
                for k in range(2):
                    sp.wait_ge(s_ust[k], g * 32 + 32)
                for q in range(4):
                    load_u(sp, g, q)
                for b in range(NBLK):
                    sp.wait_ge(s_mul, g * 8 + (NBLK + b + 1))
                    sp.dma_start(columns(net.gate1, g, b), gb[:, b % 2]).then_inc(s_gst[b % 2], 16)
                for q in range(CH):
                    if q + 4 < CH:
                        sp.wait_ge(s_ulo, g * CH + (q + 1))
                        load_u(sp, g, q + 4)
                    sp.wait_ge(s_z, g * CH + (q + 1))
                    sp.dma_start(net.z_chunks[bass.ds(g * CH + q, 1)].rearrange("a p n -> p (a n)"),
                                 zb[:, q % 2]).then_inc(s_zst[q % 2], 16)

            loop(sp, body)
            for k in range(2):
                sp.wait_ge(s_gst[k], 32 * GROUPS)
                sp.wait_ge(s_zst[k], 64 * GROUPS)

        def w_high(act, g, s, first):
            act.wait_ge(s_w[s], g * 16 + 16)
            if not first:
                if s == G:
                    act.wait_ge(s_g, g * NBLK)
                else:
                    act.wait_ge(s_ab, g * 2 * NBLK)
            nc.scalar.activation(whi[:, s], wst[:, s], ACT.Copy).then_inc(s_whi, 1)

        @block.scalar
        def _(act):
            for s in (B, A):
                w_high(act, 0, s, True)

            def sigmoid(g, n, src, first):
                if not first or n >= 2:
                    act.wait_ge(s_mul, g * 8 + (n - 1))
                nc.scalar.activation(sig[:, n % 2], src, ACT.Sigmoid).then_inc(s_sig, 1)

            def body(g, first, last):
                for b in range(NBLK):
                    act.wait_ge(s_ab, g * 8 + (2 * b + 1))
                    sigmoid(g, b, ps[:, 2 * b % 6], first)
                    if b == 0:
                        w_high(act, g, G, first)
                if not last:
                    for s in (B, A):
                        w_high(act, g + 1, s, False)
                act.wait_ge(s_taps, g * 16 + 16)
                if not first:
                    act.wait_ge(s_bhi, g * CH)
                nc.scalar.activation(thi[:], taps[:], ACT.Copy).then_inc(s_thi, 1)
                for b in range(NBLK):
                    act.wait_ge(s_g, g * 4 + (b + 1))
                    sigmoid(g, NBLK + b, ps[:, (8 + b) % 6], False)
                if first:
                    act.wait_ge(s_const, 32)
                    act.wait_ge(s_pad, 1)
                for q in range(CH + 1):
                    if q < CH:
                        act.wait_ge(s_raw[q % 4], g * 32 + 16 * (q // 4 + 1))
                        if not first or q >= 2:
                            act.wait_ge(s_cv, g * CH + (q - 1))
                        nc.scalar.activation(uhi[:, q % 2, HALO:HALO + NCOL], raw[:, q % 4], ACT.Copy).then_inc(s_uhi, 1)
                    if q:
                        c = q - 1
                        act.wait_ge(s_cv, g * CH + (c + 1))
                        if not first or c >= 2:
                            act.wait_ge(s_zst[c % 2], g * 64 + 16 * (c // 2))
                        nc.scalar.activation(zb[:, c % 2], ps[:, 6 + c % 2, 0:NCOL], ACT.Identity,
                                             bias=bdw[:, bass.ds(g * CH + c, 1)]).then_inc(s_z, 1)

            loop(act, body)

        @block.vector
        def _(dve):
            nc.vector.memset(uhi[:].bitcast(F32), 0.0)
            nc.vector.memset(ulo[:].bitcast(F32), 0.0).then_inc(s_pad, 1)

            def w_low(g, s):
                dve.wait_ge(s_whi, g * 3 + (s + 1))
                nc.vector.tensor_tensor(wlo[:, s], wst[:, s], whi[:, s].bitcast(F32), ALU.subtract).then_inc(s_wlo, 1)

            def product(g, n, dst, src, stored):
                dve.wait_ge(s_sig, g * 8 + (n + 1))
                if stored is not None:
                    dve.wait_ge(*stored)
                nc.vector.tensor_tensor(dst.rearrange("p s n -> p n s"), src.rearrange("p (n s) -> p n s", s=PHASES),
                                        sig[:, n % 2].rearrange("p (n s) -> p n s", s=PHASES),
                                        ALU.mult).then_inc(s_mul, 1)

            def body(g, first, last):
                for b in range(NBLK):
                    dve.wait_ge(s_ab, g * 8 + (2 * b + 2))
                    product(g, b, ub[:, b % 2], ps[:, (2 * b + 1) % 6],
                            None if first and b < 2 else (s_ust[b % 2], g * 32 + 16 * (b // 2)))
                    if b == 0:
                        w_low(g, G)
                if not last:
                    for s in (B, A):
                        w_low(g + 1, s)
                dve.wait_ge(s_thi, g + 1)
                if not first:
                    dve.wait_ge(s_blo, g * CH)
                nc.vector.tensor_tensor(tlo[:], taps[:], thi[:].bitcast(F32), ALU.subtract).then_inc(s_tlo, 1)
                for b in range(NBLK):
                    product(g, NBLK + b, gb[:, b % 2], ps[:, (8 + b) % 6],
                            None if first and b < 2 else (s_gst[b % 2], g * 32 + 16 * (b // 2)))
                if first:
                    dve.wait_ge(s_const, 32)
                for q in range(CH):
                    if not first or q >= 2:
                        dve.wait_ge(s_cv, g * CH + (q - 1))
                    nc.vector.tensor_tensor(bhi[:, q % 2], *banded(thi[:, q].bitcast(F32)), ALU.mult).then_inc(s_bhi, 1)
                    dve.wait_ge(s_uhi, g * CH + (q + 1))
                    nc.vector.tensor_tensor(ulo[:, q % 2, HALO:HALO + NCOL], raw[:, q % 4],
                                            uhi[:, q % 2, HALO:HALO + NCOL].bitcast(F32),
                                            ALU.subtract).then_inc(s_ulo, 1)

            for s in (B, A):
                w_low(0, s)
            loop(dve, body)

        @block.tensor
        def _(pe):
            def product(g, s, bank, b):
                for k in range(KD):
                    cols = slice(b * BLK, (b + 1) * BLK)
                    mm = split3(nc, ps[:, bank], whi[:, s, k * P:(k + 1) * P], wlo[:, s, k * P:(k + 1) * P],
                                hhi[:, k, cols], hlo[:, k, cols], k == 0, k == KD - 1)
                return mm

            def body(g, first, last):
                for b in range(NBLK):
                    for s in (B, A):
                        n = 2 * b + s
                        if b == 0:
                            pe.wait_ge(s_wlo, g * 3 + (s + 1))
                        if n >= 6:
                            if s == B:
                                pe.wait_ge(s_sig, g * 8 + (b - 3 + 1))
                            else:
                                pe.wait_ge(s_mul, g * 8 + (b - 3 + 1))
                        elif not first:
                            if n == 0:
                                pe.wait_ge(s_sig, (g - 1) * 8 + 4)
                            else:
                                pe.wait_ge(s_mul, (g - 1) * 8 + (n + 3))
                        product(g, s, n % 6, b).then_inc(s_ab, 1)
                pe.wait_ge(s_wlo, g * 3 + 3)
                for b in range(NBLK):
                    n = 8 + b
                    if (n - 6) % 2 == 0:
                        pe.wait_ge(s_sig, g * 8 + ((n - 6) // 2 + 1))
                    else:
                        pe.wait_ge(s_mul, g * 8 + ((n - 6) // 2 + 1))
                    product(g, G, n % 6, b).then_inc(s_g, 1)
                for q in range(CH):
                    pe.wait_ge(s_ulo, g * CH + (q + 1))
                    pe.wait_ge(s_bhi, g * CH + (q + 1))
                    pe.wait_ge(s_blo, g * CH + (q + 1))
                    if not first or q >= 2:
                        pe.wait_ge(s_z, g * CH + (q - 1))
                    for j in range(OFFS):
                        w = [t[:, q % 2, j].rearrange("p c f -> p (c f)") for t in (bhi, blo)]
                        mm = split3(nc, ps[:, 6 + q % 2, 0:NCOL], w[0], w[1], uhi[:, q % 2, j:j + NCOL],
                                    ulo[:, q % 2, j:j + NCOL], j == 0, j == OFFS - 1)
                    mm.then_inc(s_cv, 1)

            loop(pe, body)

        @block.gpsimd
        def _(pool):
            def body(g, first, last):
                if first:
                    pool.wait_ge(s_const, 32)
                pool.wait_ge(s_tlo, g + 1)
                for q in range(CH):
                    if not first or q >= 2:
                        pool.wait_ge(s_cv, g * CH + (q - 1))
                    nc.gpsimd.tensor_tensor(blo[:, q % 2], *banded(tlo[:, q]), ALU.mult).then_inc(s_blo, 1)

            loop(pool, body)


def conv_out(nc, net):
    FP, FN = 4, 64
    W = FP * FN
    TB = W // P
    NB = SEQ // W
    with nc.cleanup_on_exit(), ExitStack() as st:
        sb = lambda n, s, d=F32: st.enter_context(nc.sbuf_tensor("co_" + n, s, d))
        wst = sb("w", [P, 2, D])
        whi, wlo = sb("whi", [P, KD, D], F32R), sb("wlo", [P, KD, D], F32R)
        z, gt = sb("z", [P, 2, KD, FP, FN]), sb("gt", [P, 2, KD, FP, FN])
        sq = sb("sq", [P, KD, W])
        mu, rs = sb("mu", [P, W]), sb("rs", [P, W])
        v = sb("v", [P, KD, W])
        vhi, vlo = sb("vhi", [P, 2, KD, W], F32R), sb("vlo", [P, 2, KD, W], F32R)
        gln, bln = sb("gln", [P, KD]), sb("bln", [P, KD])
        xt = sb("x", [P, 2, D])
        gp, tmp, junk = sb("gp", [P, D]), sb("tmp", [P, D]), sb("junk", [P, D])
        ob = sb("ob", [P, 2, D])
        ss, rr = sb("ss", [P, 4]), sb("rr", [P, 4])
        ps = st.enter_context(nc.psum_tensor("co_ps", [P, 2, D], F32))
        pmu = st.enter_context(nc.psum_tensor("co_pmu", [P, BLK], F32))
        pvar = st.enter_context(nc.psum_tensor("co_pvar", [P, BLK], F32))
        s_w, s_z, s_gt = net.sems("co_w_in", 2), net.sems("co_z_in", 2), net.sems("co_gt_in", 2)
        s_x, s_st = net.sems("co_x_in", 2), net.sems("co_stored", 2)
        (s_const, s_whi, s_wlo, s_mean, s_mu, s_zc, s_sq, s_var, s_zn, s_sg, s_v, s_vg, s_vhi, s_vlo, s_y, s_ss, s_tmp,
         s_out, s_chain, s_rt, s_rs, s_mr, s_rr) = (net.sem("co_" + n) for n in (
             "const", "whi", "wlo", "mean", "mu", "zc", "sq", "var", "zn", "sg", "v", "vg", "vhi", "vlo", "y", "ss",
             "tmp", "out", "chain", "rt", "rs", "mr", "rr"))
        block = st.enter_context(nc.Block())

        def loop(eng, body):
            body(0, True, False)
            with eng.Fori(1, NB // 2 - 1) as i:
                body(i, False, False)
            body(NB // 2 - 1, False, True)

        def nxt(i, r):
            return (i, 1) if r == 0 else (i + 1, 0)

        def static(i, r):
            return isinstance(i, int) and 2 * i + r < 2

        def flat(t):
            return t.rearrange("p k f n -> p k (f n)")

        def load_zg(sp, i, r):
            for g in range(KD):
                for dst, src, sem in ((z, net.z_phases, s_z), (gt, net.gate1, s_gt)):
                    sp.dma_start(dst[:, r, g], src[g, :, FP * r:FP * r + FP, bass.ds(i * FN, FN)]).then_inc(sem[r], 16)

        def rows(dram, i, r, u, f):
            return dram.rearrange("(n s) d -> s n d", s=PHASES)[FP * r + 2 * u + f, bass.ds(i * FN, FN), :]

        @block.sync
        def _(sp):
            def load_x(i, r, u):
                for f in range(2):
                    sp.dma_start(xt[f * FN:(f + 1) * FN, u], rows(net.x1, i, r, u, f)).then_inc(s_x[u], 16)

            load_zg(sp, 0, 0)
            for dst, src in ((gln[:], net.g_ln), (bln[:], net.b_ln), (gp[:], net.gp_flat[1:2, :].to_broadcast([P, D]))):
                sp.dma_start(dst, src).then_inc(s_const, 16)
            for k in range(KD):
                if k >= 2:
                    sp.wait_ge(s_wlo, k - 1)
                sp.dma_start(wst[:, k % 2], net.w_o1[:, k]).then_inc(s_w[k % 2], 16)
            load_zg(sp, 0, 1)
            for u in range(TB):
                load_x(0, 0, u)

            def body(i, first, last):
                for r in range(2):
                    if not last:
                        sp.wait_ge(s_vg, i * 2 + (r + 1))
                        load_zg(sp, i + 1, r)
                    for u in range(TB):
                        sp.wait_ge(s_out, i * 4 + (2 * r + u + 1))
                        for f in range(2):
                            sp.dma_start(rows(net.out, i, r, u, f), ob[f * FN:(f + 1) * FN, u]).then_inc(s_st[u], 16)
                        if not (last and r):
                            load_x(*nxt(i, r), u)

            loop(sp, body)
            for u in range(2):
                sp.wait_ge(s_st[u], 32 * NB)

        @block.scalar
        def _(act):
            def mean(i, r):
                act.wait_ge(s_mean, i * 2 + (r + 1))
                nc.scalar.activation(mu[:], pmu[:, 0:W], ACT.Copy, scale=1.0 / D).then_inc(s_mu, 1)
                act.wait_ge(s_zc, i * 2 + (r + 1))
                nc.scalar.activation(sq[:], flat(z[:, r]), ACT.Square).then_inc(s_sq, 1)

            def root(i, r):
                act.wait_ge(s_var, i * 2 + (r + 1))
                if not static(i, r) or r:
                    act.wait_ge(s_zn, i * 2 + r)
                root_mean(nc, net, rs[:], pvar[:, 0:W], D).then_inc(s_rt, 1)

            def silu_part(i, r):
                act.wait_ge(s_zn, i * 2 + (r + 1))
                for k in range(KD):
                    nc.scalar.activation(sq[:, k], z[:, r, k].rearrange("p f n -> p (f n)"), ACT.Sigmoid,
                                         scale=gln[:, k:k + 1], bias=bln[:, k:k + 1]).then_inc(s_sg, 1)

            def high(i, r):
                act.wait_ge(s_vg, i * 2 + (r + 1))
                if not static(i, r):
                    act.wait_ge(s_y, i * 4 + 2 * (r - 1))
                nc.scalar.activation(vhi[:, r], v[:], ACT.Copy).then_inc(s_vhi, 1)

            def stat(i, r, u):
                s = 2 * r + u
                act.wait_ge(s_y, i * 4 + (s + 1))
                if not isinstance(i, int) or i:
                    act.wait_ge(s_tmp, i * 4 + (s - 3))
                nc.scalar.activation(junk[:], ps[:, u], ACT.Square, accum_out=ss[:, s:s + 1]).then_inc(s_ss, 1)
                act.wait_ge(s_ss, i * 4 + (s + 1))
                root_mean(nc, net, rr[:, s:s + 1], ss[:, s:s + 1], D).then_inc(s_mr, 1)

            act.wait_ge(s_const, 48)
            mean(0, 0)
            root(0, 0)
            silu_part(0, 0)
            for k in range(KD):
                act.wait_ge(s_w[k % 2], 16 * (k // 2 + 1))
                nc.scalar.activation(whi[:, k], wst[:, k % 2], ACT.Copy).then_inc(s_whi, 1)
            high(0, 0)

            def body(i, first, last):
                for r in range(2):
                    n = None if last and r else nxt(i, r)
                    if n:
                        mean(*n)
                        root(*n)
                        silu_part(*n)
                    stat(i, r, 0)
                    if n:
                        high(*n)
                    stat(i, r, 1)

            loop(act, body)

        @block.vector
        def _(dve):
            def centre(i, r):
                dve.wait_ge(s_mu, i * 2 + (r + 1))
                for sem in (s_z,):
                    dve.wait_ge(sem[r], i * (16 * KD) + 16 * KD)
                nc.vector.tensor_tensor(flat(z[:, r]), flat(z[:, r]), mu[:].unsqueeze(1).to_broadcast([P, KD, W]),
                                        ALU.subtract).then_inc(s_zc, 1)

            def normalise(i, r):
                link = Chain(dve, s_chain, i * (2 * KD) + r * KD)
                dve.wait_ge(s_rt, i * 2 + (r + 1))
                nc.vector.reciprocal(rs[:], rs[:]).then_inc(s_rs, 1)
                dve.wait_ge(s_rs, i * 2 + (r + 1))
                nc.vector.tensor_tensor(flat(z[:, r]), flat(z[:, r]), rs[:].unsqueeze(1).to_broadcast([P, KD, W]),
                                        ALU.mult).then_inc(s_zn, 1)
                dve.wait_ge(s_zn, i * 2 + (r + 1))
                if not static(i, r) or r:
                    dve.wait_ge(s_vlo, i * 2 + r)
                for k in range(KD):
                    link(nc.vector.tensor_scalar(v[:, k], z[:, r, k].rearrange("p f n -> p (f n)"), gln[:, k:k + 1],
                                                 bln[:, k:k + 1], ALU.mult, ALU.add))
                dve.wait_ge(s_sg, i * (2 * KD) + (KD * r + KD))
                nc.vector.tensor_tensor(v[:], v[:], sq[:], ALU.mult).then_inc(s_v, 1)

            def low(i, r):
                dve.wait_ge(s_vhi, i * 2 + (r + 1))
                nc.vector.tensor_tensor(vlo[:, r], v[:], vhi[:, r].bitcast(F32), ALU.subtract).then_inc(s_vlo, 1)

            def residual(i, r, u):
                s = 2 * r + u
                dve.wait_ge(s_mr, i * 4 + (s + 1))
                nc.vector.reciprocal(rr[:, s:s + 1], rr[:, s:s + 1]).then_inc(s_rr, 1)
                dve.wait_ge(s_rr, i * 4 + (s + 1))
                nc.vector.scalar_tensor_tensor(out=tmp[:], in0=ps[:, u], scalar=rr[:, s:s + 1], in1=gp[:],
                                               op0=ALU.mult, op1=ALU.mult).then_inc(s_tmp, 1)
                dve.wait_ge(s_tmp, i * 4 + (s + 1))
                dve.wait_ge(s_x[u], i * 64 + 32 * (r + 1))
                if not (isinstance(i, int) and i == 0 and r == 0):
                    dve.wait_ge(s_st[u], i * 64 + 32 * r)
                nc.vector.tensor_tensor(ob[:, u], tmp[:], xt[:, u], ALU.add).then_inc(s_out, 1)

            dve.wait_ge(s_const, 48)
            centre(0, 0)
            normalise(0, 0)
            for k in range(KD):
                dve.wait_ge(s_whi, k + 1)
                nc.vector.tensor_tensor(wlo[:, k], wst[:, k % 2], whi[:, k].bitcast(F32),
                                        ALU.subtract).then_inc(s_wlo, 1)
            low(0, 0)

            def body(i, first, last):
                for r in range(2):
                    n = None if last and r else nxt(i, r)
                    if n:
                        centre(*n)
                        normalise(*n)
                    residual(i, r, 0)
                    if n:
                        low(*n)
                    residual(i, r, 1)

            loop(dve, body)

        @block.tensor
        def _(pe):
            def channel_sum(dst, src):
                for k in range(KD):
                    mm = nc.tensor.matmul(dst[:, 0:W], net.ones[:], src[:, k], start=(k == 0), stop=(k == KD - 1))
                return mm

            def mean_sum(i, r):
                pe.wait_ge(s_z[r], i * (16 * KD) + 16 * KD)
                channel_sum(pmu, flat(z[:, r])).then_inc(s_mean, 1)

            def var_sum(i, r):
                pe.wait_ge(s_sq, i * 2 + (r + 1))
                channel_sum(pvar, sq[:]).then_inc(s_var, 1)

            mean_sum(0, 0)
            var_sum(0, 0)

            def body(i, first, last):
                for r in range(2):
                    n = None if last and r else nxt(i, r)
                    if n:
                        mean_sum(*n)
                    pe.wait_ge(s_vlo, i * 2 + (r + 1))
                    for u in range(TB):
                        s = 2 * r + u
                        if not (first and r == 0):
                            pe.wait_ge(s_tmp, i * 4 + (s - 1))
                        tok = slice(u * P, (u + 1) * P)
                        for h in range(2):
                            c = slice(h * BLK, (h + 1) * BLK)
                            for k in range(KD):
                                if first and s == 0 and h == 0:
                                    pe.wait_ge(s_wlo, k + 1)
                                mm = split3(nc, ps[:, u, c], vhi[:, r, k, tok], vlo[:, r, k, tok],
                                            whi[:, k, c], wlo[:, k, c], k == 0, k == KD - 1)
                            if u == 0 and h == 0 and n:
                                var_sum(*n)
                        mm.then_inc(s_y, 1)

            loop(pe, body)

        @block.gpsimd
        def _(pool):
            def gate(i, r):
                pool.wait_ge(s_v, i * 2 + (r + 1))
                pool.wait_ge(s_gt[r], i * (16 * KD) + 16 * KD)
                nc.gpsimd.tensor_tensor(v[:], v[:], flat(gt[:, r]), ALU.mult).then_inc(s_vg, 1)

            gate(0, 0)

            def body(i, first, last):
                for r in range(2):
                    n = None if last and r else nxt(i, r)
                    if n:
                        gate(*n)

            loop(pool, body)


def build(nc, io, out):
    with ExitStack() as stack:
        net = Net(nc, stack)
        sb = lambda n, s, d=F32: stack.enter_context(nc.sbuf_tensor(n, s, d))
        scratch = lambda n, s: nc.dram_tensor(n, s, F32, kind="Internal").ap()
        net.x, net.ctx, net.c_cols, net.out = io["x"], io["ctx"], io["c_cols"], out
        net.w_mod, net.b_mod, net.g_pre, net.g_post = io["w_mod"], io["b_mod"], io["g_pre"], io["g_post"]
        net.w_in, net.g_q, net.g_kv, net.w_uq, net.w_ukv = (io[n] for n in ("w_in", "g_q", "g_kv", "w_uq", "w_ukv"))
        net.w_o0, net.cv_w_in, net.taps, net.b_dw = io["w_o0"], io["cv_w_in"], io["taps"], io["b_dw"]
        net.g_ln, net.b_ln, net.w_o1 = io["g_ln"], io["b_ln"], io["w_o1"]
        net.ident_in, net.perm_in, net.mask_in, net.rope_tab = io["ident"], io["perm"], io["mask"], io["rope_tab"]

        net.raw = scratch("raw_latents", [KQ + KKV + 1, P, TOK])
        net.gate0 = scratch("silu_gate0", [HEADS, P, SEQ])
        net.qn = scratch("q_nope", [HEADS, P, SEQ])
        net.qr = scratch("q_rope", [HEADS // 2, P, SEQ])
        net.qr_heads = net.qr.rearrange("t (e p) n -> (t e) p n", e=2)
        net.kn = scratch("k_nope", [HEADS, P, TOK])
        net.kr = scratch("k_rope", [P, TOK])
        net.v = scratch("values", [NKT, P, HEADS * VDIM])
        net.og = scratch("attn_gated", [HEADS, P, SEQ])
        net.x1 = scratch("x1", [SEQ, D])
        net.u_phases = scratch("u_phases", [KD, P, PHASES, NCOL])
        net.u_chunks = net.u_phases.rearrange("g (q c) s n -> (g q) (c s) n", c=CCH)
        net.z_phases = scratch("z_phases", [KD, P, PHASES, NCOL])
        net.z_chunks = net.z_phases.rearrange("g (q c) s n -> (g q) (c s) n", c=CCH)
        net.gate1 = scratch("silu_gate1", [KD, P, PHASES, NCOL])
        net.gp_row = scratch("gate_rows", [2 * KD, P])
        net.gp_flat = net.gp_row.rearrange("(l k) p -> l (k p)", l=2)

        net.ident, net.perm, net.ones = sb("ident", [P, P]), sb("perm", [P, P]), sb("ones", [P, P])
        net.eps = sb("eps", [P, 1])
        net.mod = sb("mod", [P, 6 * KD, 2])
        net.amul = sb("amul", [P, 2, KD, 2])

        modulation(nc, net)
        with ExitStack() as st:
            hhi = st.enter_context(nc.sbuf_tensor("h0hi", [P, KD, TOK], F32R))
            hlo = st.enter_context(nc.sbuf_tensor("h0lo", [P, KD, TOK], F32R))
            hidden(nc, net, 0, net.x, net.ctx, hhi, hlo)
            in_proj(nc, net, hhi, hlo)
        latents(nc, net, "q")
        latents(nc, net, "kv")
        attention(nc, net)
        attn_out(nc, net)
        with ExitStack() as st:
            hhi = st.enter_context(nc.sbuf_tensor("h1hi", [P, KD, SEQ], F32R))
            hlo = st.enter_context(nc.sbuf_tensor("h1lo", [P, KD, SEQ], F32R))
            hidden(nc, net, 1, net.x1, None, hhi, hlo)
            conv_in(nc, net, hhi, hlo)
        conv_out(nc, net)


def constants():
    half = ROPE // 2
    freqs = (1.0 / (np.float32(10000.0) ** (np.arange(0, half, 2, dtype=np.float32) / np.float32(half)))).astype(
        np.float32)
    pos = np.arange(SEQ)
    ang = [(p.astype(np.float32)[None, :] * freqs[:, None]).astype(np.float32) for p in (pos // GRID_W, pos % GRID_W)]
    tab = np.zeros((2, ROPE, TOK), np.float32)
    tab[0, :, SEQ:] = 1.0
    for a in range(2):
        for h in range(2):
            rows = slice(a * half + h * half // 2, a * half + (h + 1) * half // 2)
            tab[0, rows, :SEQ], tab[1, rows, :SEQ] = np.cos(ang[a]), np.sin(ang[a])
    perm = np.zeros((P, P), np.float32)
    for m in range(P):
        if m % half < half // 2:
            perm[m + half // 2, m] = -1.0
        else:
            perm[m - half // 2, m] = 1.0
    mask = (np.arange(P)[:, None] // PHASES == np.arange(CCH)[None, :]).astype(np.float32)
    return {"rope_tab": np.tile(tab, (1, 2, 1)), "perm": perm, "mask": mask, "ident": np.eye(P, dtype=np.float32)}


def layout(i):
    a = {k: np.asarray(v) for k, v in i.items()}
    tiles = lambda w: w.reshape(w.shape[0] // P, P, -1, P).transpose(2, 1, 0, 3)
    cols = lambda w: w.reshape(-1, P).T
    out = {"x": a["x"][0], "ctx": a["ctx"][0]}
    out["c_cols"] = np.stack([cols(a["c"][0]), cols(a["c_ctx"])], axis=2)
    out["w_mod"] = np.concatenate([tiles(a["w_mod"][l]) for l in range(2)])
    out["b_mod"] = cols(a["b_mod"].reshape(-1))
    out["g_pre"], out["g_post"] = (a[n].reshape(2, KD, P).transpose(2, 0, 1) for n in ("g_pre", "g_post"))
    w = a["mla_w_in"][0]
    rope0 = QL + KVL
    w = np.concatenate([w[:, :rope0], w[:, rope0:rope0 + ROPE], w[:, rope0:rope0 + ROPE], w[:, rope0 + ROPE:]], axis=1)
    out["w_in"] = tiles(w).reshape(-1, P, D)
    out["g_q"], out["g_kv"] = cols(a["mla_g_q"][0]), cols(a["mla_g_kv"][0])
    w = a["mla_w_uq"][0].reshape(QL, HEADS, NOPE + ROPE)
    w = np.concatenate([w[:, :, NOPE:].reshape(QL, -1), w[:, :, :NOPE].reshape(QL, -1)], axis=1)
    out["w_uq"] = w.reshape(KQ, P, -1).transpose(1, 0, 2)
    w = a["mla_w_ukv"][0].reshape(KVL, HEADS, NOPE + VDIM)
    w = np.concatenate([w[:, :, :NOPE].reshape(KVL, -1), w[:, :, NOPE:].reshape(KVL, -1)], axis=1)
    out["w_ukv"] = w.reshape(KKV, P, -1).transpose(1, 0, 2)
    out["w_o0"], out["w_o1"] = (a[n][0].reshape(KD, P, D).transpose(1, 0, 2) for n in ("mla_w_o", "cv_w_o"))
    w = a["cv_w_in"][0].reshape(D, 3, KD, P)[:, [1, 0, 2]].transpose(0, 2, 1, 3).reshape(D, -1)
    out["cv_w_in"] = tiles(w).reshape(-1, P, D)
    dw = a["cv_w_dw"][0][:, 0, :]
    taps = np.zeros((D, PHASES, OFFS, PHASES), np.float32)
    for s in range(PHASES):
        for j in range(OFFS):
            for f in range(PHASES):
                t = PHASES * (j - OFFS // 2) + s - f + PAD
                if 0 <= t < CONV_K:
                    taps[:, s, j, f] = dw[t]
    out["taps"] = taps.reshape(KD, P // CCH, P, OFFS * PHASES).transpose(0, 2, 1, 3)
    out["b_dw"] = np.repeat(a["cv_b_dw"][0].reshape(-1, CCH), PHASES, axis=1).T
    out["g_ln"], out["b_ln"] = cols(a["cv_g_ln"][0]), cols(a["cv_b_ln"][0])
    out.update(constants())
    return {k: np.ascontiguousarray(v) for k, v in out.items()}


def kernel(**inputs):
    import concourse.bacc as bacc
    from concourse.bass_utils import run_bass_kernel_spmd

    arrays = layout(inputs)
    nc = bacc.Bacc("TRN2", target_bir_lowering=False, num_devices=1)
    io = {k: nc.dram_tensor(f"in_{k}", v.shape, F32, kind="ExternalInput").ap() for k, v in arrays.items()}
    out = nc.dram_tensor("out_x", (SEQ, D), F32, kind="ExternalOutput").ap()
    build(nc, io, out)
    r = run_bass_kernel_spmd(nc, [{f"in_{k}": v for k, v in arrays.items()}], core_ids=[0])
    return r.results[0]["out_x"].reshape(1, SEQ, D)
```

```python
from contextlib import ExitStack

import numpy as np

import concourse.bass as bass
from concourse import mybir

F32 = mybir.dt.float32
F32R = mybir.dt.float32r
ALU = mybir.AluOpType
ACT = mybir.ActivationFunctionType
AXX = mybir.AxisListType.X

P = 128
D = 1024
KD = D // P
SEQ, CTX = 2048, 256
TOK = SEQ + CTX
BLK = 512
NBLK = SEQ // BLK
HEADS, NOPE, ROPE, VDIM = 8, 128, 64, 128
QL, KVL = 384, 256
KQ, KKV = QL // P, KVL // P
CONV_K, PAD = 31, 15
PHASES = 8
CCH = P // PHASES
NCOL = SEQ // PHASES
OFFS = 5
EPS = 1e-6
GRID_W = 64
SCALE = (NOPE + ROPE) ** -0.5
NKT = TOK // P
NCHUNK = 5
MOD_TILES = 2 * 3 * KD
MOD_FIRST = 2 * KD
MOD_LATER = MOD_TILES - MOD_FIRST
SLOTS = NKT + 1


def chunk(c):
    return slice(c * BLK, min((c + 1) * BLK, TOK))


class Chain:

    def __init__(self, eng, sem, base=0):
        self.eng, self.sem, self.base, self.n = eng, sem, base, 0

    def __call__(self, ins):
        self.n += 1
        ins.then_inc(self.sem, 1)
        self.eng.wait_ge(self.sem, self.base + self.n)


class Net:

    def __init__(self, nc, stack):
        self.nc, self.stack = nc, stack

    def sem(self, name):
        return self.nc.alloc_semaphore(name=name)

    def sems(self, name, n):
        return [self.sem(f"{name}{i}") for i in range(n)]


def root_mean(nc, net, out, sums, n):
    return nc.scalar.activation(out, sums, ACT.Sqrt, scale=1.0 / n, bias=net.eps[:])


def split3(nc, out, whi, wlo, xhi, xlo, first, last):
    nc.tensor.matmul(out, whi, xhi, start=first, stop=False)
    nc.tensor.matmul(out, whi, xlo, start=False, stop=False)
    return nc.tensor.matmul(out, wlo, xhi, start=False, stop=last)


def modulation(nc, net):
    R = 4
    with nc.cleanup_on_exit(), ExitStack() as st:
        sb = lambda n, s, d=F32: st.enter_context(nc.sbuf_tensor(n, s, d))
        wst = sb("mod_w", [P, R, KD, P])
        csig = sb("mod_csig", [P, KD, 2])
        acc = st.enter_context(nc.psum_tensor("mod_acc", [P, BLK], F32))
        s_small = net.sem("mod_small")
        s_w = net.sems("mod_w_in", R)
        s_sig, s_silu, s_used, s_chain = (net.sem("mod_" + n) for n in ("sig", "silu", "used", "chain"))
        mod, cc = net.mod, net.cc
        accv = acc[:, 0:2 * MOD_FIRST].rearrange("p (m s) -> p m s", s=2)
        block = st.enter_context(nc.Block())

        @block.sync
        def _(sp):
            for dst, src in ((cc, net.c_cols), (net.bm, net.b_mod), (net.gpre, net.g_pre), (net.gpost, net.g_post),
                             (net.ident, net.ident_in), (net.perm, net.perm_in)):
                sp.dma_start(dst[:], src).then_inc(s_small, 16)
            for r in range(R):
                sp.dma_start(wst[:, r], net.w_mod[r]).then_inc(s_w[r], 16)
            with sp.Fori(0, MOD_FIRST // R - 1) as i:
                for r in range(R):
                    sp.wait_ge(s_used, i * R + (r + 1))
                    sp.dma_start(wst[:, r], net.w_mod[bass.ds(i * R + (R + r), 1)].rearrange("a p k c -> p (a k) c")
                                 ).then_inc(s_w[r], 16)

        @block.scalar
        def _(act):
            act.wait_ge(s_small, 96)
            nc.scalar.activation(csig[:], cc[:], ACT.Sigmoid).then_inc(s_sig, 1)

        @block.tensor
        def _(pe):
            pe.wait_ge(s_silu, 1)
            with pe.Fori(0, MOD_FIRST // R) as i:
                for r in range(R):
                    pe.wait_ge(s_w[r], (i + 1) * 16)
                    for k in range(KD):
                        mm = nc.tensor.matmul(acc[:, bass.ds(i * (2 * R) + 2 * r, 2)], wst[:, r, k, :],
                                              cc[:, k, :], start=(k == 0), stop=(k == KD - 1))
                    mm.then_inc(s_used, 1)

        @block.vector
        def _(dve):
            nc.vector.memset(net.eps[:], EPS)
            nc.vector.memset(net.ones[:], 1.0)
            link = Chain(dve, s_chain)
            dve.wait_ge(s_small, 96)
            dve.wait_ge(s_sig, 1)
            nc.vector.tensor_tensor(cc[:], cc[:], csig[:], ALU.mult).then_inc(s_silu, 1)
            dve.wait_ge(s_used, MOD_FIRST)
            link(nc.vector.tensor_tensor(mod[:, 0:MOD_FIRST], accv,
                                         net.bm[:, 0:MOD_FIRST].unsqueeze(2).to_broadcast([P, MOD_FIRST, 2]), ALU.add))
            scale_rows(nc, net, 0, 2)


def scale_rows(nc, net, l, streams):
    scale = 3 * KD * l + KD
    return nc.vector.scalar_tensor_tensor(
        out=net.amul[:, l, :, 0:streams], in0=net.mod[:, scale:scale + KD, 0:streams], scalar=1.0,
        in1=net.gpre[:, l].unsqueeze(2).to_broadcast([P, KD, streams]), op0=ALU.add, op1=ALU.mult)


def hidden(nc, net, layer, x_dram, ctx_dram, hhi, hlo):
    tag = f"hid{layer}_"
    R = BLK // P
    blocks = [(x_dram, b * BLK, R, 0) for b in range(NBLK)]
    if ctx_dram is not None:
        blocks.append((ctx_dram, 0, CTX // P, 1))
    first_tile = [sum(t for _, _, t, _ in blocks[:b]) for b in range(len(blocks) + 1)]
    with nc.cleanup_on_exit(), ExitStack() as st:
        sb = lambda n, s, d=F32: st.enter_context(nc.sbuf_tensor(tag + n, s, d))
        xt = sb("x", [P, 2, R, D])
        junk = sb("junk", [P, D])
        tmp = sb("tmp", [P, KD, BLK])
        ss = sb("ss", [P, 2, R])
        rs = sb("rs", [P, 2, R])
        ps = st.enter_context(nc.psum_tensor(tag + "ps", [P, KD, BLK], F32))
        s_x = net.sems(tag + "x_in", 2 * R)
        s_ss, s_rt, s_rs, s_xrv, s_xrg, s_tile, s_tr, s_h, s_hi, s_lo = (
            net.sem(tag + n) for n in ("ss", "rt", "rs", "xrv", "xrg", "tile", "tr", "h", "hi", "lo"))
        mod, amul = net.mod, net.amul
        block = st.enter_context(nc.Block())

        @block.sync
        def _(sp):
            for b, (src, row, tiles, _) in enumerate(blocks):
                for r in range(tiles):
                    if b >= 2:
                        if r < R - 1:
                            sp.wait_ge(s_tile, (b - 2) * (R - 1) + r + 1)
                        else:
                            sp.wait_ge(s_tr, (b - 1) * KD)
                    sp.dma_start(xt[:, b % 2, r], src[row + r * P:row + (r + 1) * P, :]).then_inc(
                        s_x[b % 2 * R + r], 16)

        @block.scalar
        def _(act):
            def statistics(b):
                tiles, u = blocks[b][2], b % 2
                if b >= 2:
                    act.wait_ge(s_rs, b - 1)
                for r in range(tiles):
                    act.wait_ge(s_x[u * R + r], (b // 2 + 1) * 16)
                    if b or r:
                        act.wait_ge(s_ss, first_tile[b] + r)
                    nc.scalar.activation(junk[:], xt[:, u, r], ACT.Square, accum_out=ss[:, u, r:r + 1]).then_inc(
                        s_ss, 1)
                act.wait_ge(s_ss, first_tile[b + 1])
                if b >= 2:
                    act.wait_ge(s_xrv, first_tile[b - 1] // 2)
                    act.wait_ge(s_xrg, first_tile[b - 1] // 2)
                root_mean(nc, net, rs[:, u, 0:tiles], ss[:, u, 0:tiles], D).then_inc(s_rt, 1)

            def modulated(b):
                _, _, tiles, stream = blocks[b]
                for k in range(KD):
                    act.wait_ge(s_tr, b * KD + k + 1)
                    if b:
                        act.wait_ge(s_lo, (b - 1) * KD + k + 1)
                    nc.scalar.activation(tmp[:, k, 0:tiles * P], ps[:, k, 0:tiles * P], ACT.Identity,
                                         scale=amul[:, layer, k, stream:stream + 1],
                                         bias=mod[:, 3 * KD * layer + k, stream:stream + 1]).then_inc(s_h, 1)

            statistics(0)
            for b in range(len(blocks)):
                if b + 1 < len(blocks):
                    statistics(b + 1)
                modulated(b)

        def normalise(eng, b, r):
            return eng.tensor_scalar(xt[:, b % 2, r], xt[:, b % 2, r], rs[:, b % 2, r:r + 1], None, ALU.mult)

        @block.vector
        def _(dve):
            def inverse(b):
                dve.wait_ge(s_rt, b + 1)
                r = rs[:, b % 2, 0:blocks[b][2]]
                nc.vector.reciprocal(r, r).then_inc(s_rs, 1)

            def normalised(b, r):
                dve.wait_ge(s_rs, b + 1)
                normalise(nc.vector, b, r).then_inc(s_xrv, 1)

            inverse(0)
            for r in range(0, R, 2):
                normalised(0, r)
            for b, (_, _, tiles, _) in enumerate(blocks):
                nxt = b + 1 if b + 1 < len(blocks) else None
                for k in range(KD):
                    h, l = (t[:, k, b * BLK:b * BLK + tiles * P] for t in (hhi, hlo))
                    t = tmp[:, k, 0:tiles * P]
                    if nxt and k == 0:
                        inverse(nxt)
                    if nxt and k in (0, 2) and k < blocks[nxt][2]:
                        normalised(nxt, k)
                    dve.wait_ge(s_h, b * KD + k + 1)
                    nc.vector.tensor_copy(h, t).then_inc(s_hi, 1)
                    dve.wait_ge(s_hi, b * KD + k + 1)
                    nc.vector.tensor_tensor(l, t, h.bitcast(F32), ALU.subtract).then_inc(s_lo, 1)

        @block.gpsimd
        def _(pool):
            for b, (_, _, tiles, _) in enumerate(blocks):
                pool.wait_ge(s_rs, b + 1)
                for r in range(1, tiles, 2):
                    normalise(nc.gpsimd, b, r).then_inc(s_xrg, 1)

        @block.tensor
        def _(pe):
            for b, (_, _, tiles, _) in enumerate(blocks):
                for r in range(tiles):
                    pe.wait_ge(s_xrg if r % 2 else s_xrv, (first_tile[b] + r) // 2 + 1)
                    for k in range(KD):
                        if r == 0 and b:
                            pe.wait_ge(s_h, (b - 1) * KD + k + 1)
                        t = nc.tensor.transpose(ps[:, k, r * P:(r + 1) * P], xt[:, b % 2, r, k * P:(k + 1) * P],
                                                net.ident[:])
                        if r == tiles - 1:
                            t.then_inc(s_tr, 1)
                        elif k == KD - 1:
                            t.then_inc(s_tile, 1)


def in_proj(nc, net, hhi, hlo):
    RAW = KQ + KKV + 1
    with nc.cleanup_on_exit(), ExitStack() as st:
        sb = lambda n, s, d=F32: st.enter_context(nc.sbuf_tensor("inp_" + n, s, d))
        wst = sb("w", [P, 2, D])
        whi, wlo = sb("whi", [P, 2, D], F32R), sb("wlo", [P, 2, D], F32R)
        ob = sb("ob", [P, 4, BLK])
        sig = sb("sig", [P, 2, BLK])
        ps = st.enter_context(nc.psum_tensor("inp_ps", [P, 8, BLK], F32))
        s_w = net.sems("inp_w_in", 2)
        s_st = net.sems("inp_stored", 4)
        s_whi, s_wlo, s_out, s_sig, s_free = (net.sem("inp_" + n) for n in ("whi", "wlo", "out", "sig", "free"))
        block = st.enter_context(nc.Block())

        raw = [(m, b * BLK, BLK if b < NBLK else CTX) for m in range(RAW) for b in range(NBLK + (m >= KQ))]
        NRAW = len(raw)
        first_of = [min(i for i, o in enumerate(raw) if o[0] == m) for m in range(RAW)] + [NRAW]

        @block.sync
        def _(sp):
            for m in range(2):
                sp.dma_start(wst[:, m], net.w_in[m]).then_inc(s_w[m], 16)
            for o, (m, col, width) in enumerate(raw):
                if o == first_of[m]:
                    sp.wait_ge(s_wlo, m + 1)
                    sp.dma_start(wst[:, m % 2], net.w_in[m + 2]).then_inc(s_w[m % 2], 16)
                sp.wait_ge(s_free, o + 1)
                sp.dma_start(net.raw[m, :, col:col + width], ob[:, o % 4, 0:width]).then_inc(s_st[o % 4], 16)

            def pair(i, last):
                for r in range(2):
                    if not last:
                        sp.wait_ge(s_wlo, i * 2 + (RAW + r + 1))
                        sp.dma_start(wst[:, r], net.w_in[bass.ds(i * 2 + (RAW + r + 2), 1)].rearrange(
                            "a p n -> p (a n)")).then_inc(s_w[r], 16)
                    for b in range(NBLK):
                        o = NRAW + 4 * r + b
                        sp.wait_ge(s_free, i * 8 + (o + 1))
                        sp.dma_start(net.gate0[bass.ds(i * 2 + r, 1), :, b * BLK:(b + 1) * BLK].rearrange(
                            "a p n -> p (a n)"), ob[:, o % 4]).then_inc(s_st[o % 4], 16)

            with sp.Fori(0, HEADS // 2 - 1) as i:
                pair(i, False)
            pair(HEADS // 2 - 1, True)
            for k in range(4):
                sp.wait_ge(s_st[k], 16 * len(range(k, NRAW + HEADS * NBLK, 4)))

        def w_high(act, i, m):
            r = m % 2
            act.wait_ge(s_w[r], i * 16 + 16 * (m // 2 + 1))
            if m >= 2:
                act.wait_ge(s_out, i * 8 + (first_of[m - 1] if m <= RAW else NRAW + 4 * (m - RAW - 1)))
            nc.scalar.activation(whi[:, r], wst[:, r], ACT.Copy).then_inc(s_whi, 1)

        def w_low(dve, i, m):
            dve.wait_ge(s_whi, i * 2 + (m + 1))
            nc.vector.tensor_tensor(wlo[:, m % 2], wst[:, m % 2], whi[:, m % 2].bitcast(F32),
                                    ALU.subtract).then_inc(s_wlo, 1)

        @block.tensor
        def _(pe):
            def product(r, i, o, col, width):
                if not isinstance(i, int) or o >= 8:
                    pe.wait_ge(s_free, i * 8 + (o - 7))
                for k in range(KD):
                    mm = split3(nc, ps[:, o % 8, 0:width], whi[:, r, k * P:(k + 1) * P], wlo[:, r, k * P:(k + 1) * P],
                                hhi[:, k, col:col + width], hlo[:, k, col:col + width], k == 0, k == KD - 1)
                mm.then_inc(s_out, 1)

            for o, (m, col, width) in enumerate(raw):
                if o == first_of[m]:
                    pe.wait_ge(s_wlo, m + 1)
                product(m % 2, 0, o, col, width)
            with pe.Fori(0, HEADS // 2) as i:
                for r in range(2):
                    pe.wait_ge(s_wlo, i * 2 + (RAW + r + 1))
                    for b in range(NBLK):
                        product(r, i, NRAW + 4 * r + b, b * BLK, BLK)

        @block.scalar
        def _(act):
            w_high(act, 0, 0)
            for o, (m, col, width) in enumerate(raw):
                if o == first_of[m]:
                    w_high(act, 0, m + 1)
                act.wait_ge(s_out, o + 1)
                if o >= 4:
                    act.wait_ge(s_st[o % 4], 16 * (o // 4))
                nc.scalar.activation(ob[:, o % 4, 0:width], ps[:, o % 8, 0:width], ACT.Copy).then_inc(s_free, 1)

            def pair(i, last):
                for r in range(2):
                    if not (last and r):
                        w_high(act, i, RAW + r + 1)
                    for b in range(NBLK):
                        o = NRAW + 4 * r + b
                        act.wait_ge(s_out, i * 8 + (o + 1))
                        act.wait_ge(s_free, i * 8 + (o - 1))
                        nc.scalar.activation(sig[:, b % 2], ps[:, o % 8], ACT.Sigmoid).then_inc(s_sig, 1)

            with act.Fori(0, HEADS // 2 - 1) as i:
                pair(i, False)
            pair(HEADS // 2 - 1, True)

        @block.vector
        def _(dve):
            for m in range(RAW + 1):
                w_low(dve, 0, m)

            def pair(i, last):
                for r in range(2):
                    if not (last and r):
                        w_low(dve, i, RAW + r + 1)
                    for b in range(NBLK):
                        o = NRAW + 4 * r + b
                        dve.wait_ge(s_sig, i * 8 + (4 * r + b + 1))
                        dve.wait_ge(s_st[o % 4], i * 32 + 16 * (o // 4))
                        nc.vector.tensor_tensor(ob[:, o % 4], ps[:, o % 8], sig[:, b % 2],
                                                ALU.mult).then_inc(s_free, 1)

            with dve.Fori(0, HEADS // 2 - 1) as i:
                pair(i, False)
            pair(HEADS // 2 - 1, True)


def latents(nc, net, kind):
    isq = kind == "q"
    tag = kind + "u_"
    KC = KQ if isq else KKV
    raw0 = 0 if isq else KQ
    NROPE = HEADS // 2 if isq else 1
    blocks = [(b, b * BLK, BLK) for b in range(NBLK)] + ([] if isq else [(NBLK, SEQ, CTX)])
    ncols = HEADS * (NOPE + ROPE) if isq else HEADS * (NOPE + VDIM)

    def outputs(width):
        if isq:
            return [("rope", t, 0) for t in range(NROPE)] + [("nope", h, 0) for h in range(HEADS)]
        return [("key", h, 0) for h in range(HEADS)] + [("val", t, n) for t in range(width // P) for n in range(2)]

    NO = len(outputs(BLK))
    NW = ncols // BLK
    with nc.cleanup_on_exit(), ExitStack() as st:
        sb = lambda n, s, d=F32: st.enter_context(nc.sbuf_tensor(tag + n, s, d))
        wst = sb("w", [P, 2, KC, BLK])
        whi, wlo = sb("whi", [P, KC, ncols], F32R), sb("wlo", [P, KC, ncols], F32R)
        gain = sb("gain", [P, KC])
        xin = sb("xin", [P, 2, KC, BLK])
        krin = sb("krin", [P, 2, BLK])
        cs = sb("cs", [P, 2, 2, BLK])
        sq = sb("sq", [P, KC, BLK])
        ssum = sb("ssum", [P, BLK])
        rs = sb("rs", [P, BLK])
        xn = sb("xn", [P, KC, BLK])
        xhi, xlo = sb("xhi", [P, 2, KC, BLK], F32R), sb("xlo", [P, 2, KC, BLK], F32R)
        rq = sb("rq", [P, 2, BLK])
        t1, t2 = sb("t1", [P, BLK]), sb("t2", [P, BLK])
        ob = sb("ob", [P, 4, BLK])
        rob = sb("rob", [P, 2, BLK])
        ps = st.enter_context(nc.psum_tensor(tag + "ps", [P, 8, BLK], F32))
        SUM, PERM = 6, 7
        s_w = net.sems(tag + "w_in", 2)
        s_x = net.sems(tag + "x_in", 2)
        s_st = net.sems(tag + "stored", 4)
        s_rst = net.sems(tag + "rstored", 2)
        (s_gain, s_whi, s_wlo, s_sq, s_sum, s_ones, s_xn, s_xhi, s_xlo, s_out, s_ev, s_rq, s_perm, s_rope,
         s_rt, s_chain) = (net.sem(tag + n) for n in ("gain", "whi", "wlo", "sq", "sum", "ones", "xn", "xhi", "xlo", "out",
                                                "ev", "rq", "perm", "rope", "rt", "chain"))
        NLOAD = 3 if isq else 4
        w_dram = net.w_uq if isq else net.w_ukv
        block = st.enter_context(nc.Block())

        @block.sync
        def _(sp):
            sp.dma_start(gain[:], net.g_q if isq else net.g_kv).then_inc(s_gain, 16)

            def load(b, col, width):
                r = b % 2
                if b >= 2:
                    sp.wait_ge(s_xn, KC * (b - 1))
                    sp.wait_ge(s_rope, NROPE * (b - 1))
                sp.dma_start(xin[:, r, :, 0:width],
                             net.raw[raw0:raw0 + KC, :, col:col + width].rearrange("k p n -> p k n")).then_inc(s_x[r], 16)
                for t in range(2):
                    sp.dma_start(cs[:, r, t, 0:width], net.rope_tab[t, :, col:col + width]).then_inc(s_x[r], 16)
                if not isq:
                    sp.dma_start(krin[:, r, 0:width], net.raw[KQ + KKV, :, col:col + width]).then_inc(s_x[r], 16)

            for blk in blocks[:1]:
                load(*blk)
            for n in range(NW):
                if n >= 2:
                    sp.wait_ge(s_wlo, n - 1)
                sp.dma_start(wst[:, n % 2], w_dram[:, :, n * BLK:(n + 1) * BLK]).then_inc(s_w[n % 2], 16)
            load(*blocks[1])
            e = u = 0
            for b, col, width in blocks:
                for j, (what, t, n) in enumerate(outputs(width)):
                    if j == (NROPE if isq else 3):
                        for _ in range(NROPE):
                            sp.wait_ge(s_rope, u + 1)
                            dst = net.qr[u % NROPE, :, col:col + width] if isq else net.kr[:, col:col + width]
                            sp.dma_start(dst, rob[:, u % 2, 0:width]).then_inc(s_rst[u % 2], 16)
                            u += 1
                        if b + 2 < len(blocks):
                            load(*blocks[b + 2])
                    if what == "rope":
                        continue
                    sp.wait_ge(s_ev, NO * b + j + 1)
                    if what == "val":
                        dst = net.v[col // P + t, :, n * BLK:(n + 1) * BLK]
                    else:
                        dst = (net.qn if isq else net.kn)[t, :, col:col + width]
                    wd = BLK if what == "val" else width
                    sp.dma_start(dst, ob[:, e % 4, 0:wd]).then_inc(s_st[e % 4], 16)
                    e += 1
            for k in range(4):
                sp.wait_ge(s_st[k], 16 * len(range(k, e, 4)))
            for k in range(2):
                sp.wait_ge(s_rst[k], 16 * len(range(k, u, 2)))

        @block.scalar
        def _(act):
            def square(b, width):
                act.wait_ge(s_x[b % 2], 16 * NLOAD * (b // 2 + 1))
                if b:
                    act.wait_ge(s_sum, b)
                nc.scalar.activation(sq[:, :, 0:width], xin[:, b % 2, :, 0:width], ACT.Square).then_inc(s_sq, 1)

            def root(b, width):
                act.wait_ge(s_ones, b + 1)
                if b:
                    act.wait_ge(s_xn, KC * b)
                root_mean(nc, net, rs[:, 0:width], ps[:, SUM, 0:width], KC * P).then_inc(s_rt, 1)

            def high(b, width):
                if b >= 2:
                    act.wait_ge(s_out, NO * (b - 1))
                for k in range(KC):
                    act.wait_ge(s_xn, KC * b + k + 1)
                    nc.scalar.activation(xhi[:, b % 2, k, 0:width], xn[:, k, 0:width], ACT.Copy).then_inc(s_xhi, 1)

            square(0, BLK)
            root(0, BLK)
            for n in range(NW):
                act.wait_ge(s_w[n % 2], 16 * (n // 2 + 1))
                nc.scalar.activation(whi[:, :, n * BLK:(n + 1) * BLK], wst[:, n % 2], ACT.Copy).then_inc(s_whi, 1)
                if n == 0:
                    high(0, BLK)
            for b, col, width in blocks:
                outs = outputs(width)
                more = b + 1 < len(blocks)
                if more:
                    square(b + 1, blocks[b + 1][2])
                for j, (what, t, n) in enumerate(outs):
                    o = NO * b + j
                    act.wait_ge(s_out, o + 1)
                    wd = width if what != "val" else BLK
                    if what == "rope":
                        u = NROPE * b + t
                        if u >= 2:
                            act.wait_ge(s_rope, u - 1)
                        nc.scalar.activation(rq[:, t % 2, 0:wd], ps[:, o % 4, 0:wd], ACT.Copy).then_inc(s_rq, 1)
                        act.wait_ge(s_rq, u + 1)
                        act.sem_inc(s_ev, 1)
                    else:
                        e = o - NROPE * (b + 1) if isq else o
                        if e >= 4:
                            act.wait_ge(s_st[e % 4], 16 * (e // 4))
                        nc.scalar.activation(ob[:, e % 4, 0:wd], ps[:, o % 4, 0:wd], ACT.Copy).then_inc(s_ev, 1)
                    if j == 3 and more:
                        root(b + 1, blocks[b + 1][2])
                    if j == 6 and more:
                        high(b + 1, blocks[b + 1][2])

        @block.vector
        def _(dve):
            link = Chain(dve, s_chain)

            def norm(b, width):
                dve.wait_ge(s_sq, b + 1)
                if KC == 3:
                    link(nc.vector.tensor_tensor(ssum[:, 0:width], sq[:, 0, 0:width], sq[:, 1, 0:width], ALU.add))
                    nc.vector.tensor_tensor(ssum[:, 0:width], ssum[:, 0:width], sq[:, 2, 0:width],
                                            ALU.add).then_inc(s_sum, 1)
                else:
                    nc.vector.tensor_tensor(ssum[:, 0:width], sq[:, 0, 0:width], sq[:, 1, 0:width],
                                            ALU.add).then_inc(s_sum, 1)

            def scale(b, width):
                dve.wait_ge(s_rt, b + 1)
                link(nc.vector.reciprocal(rs[:, 0:width], rs[:, 0:width]))
                for k in range(KC):
                    nc.vector.scalar_tensor_tensor(out=xn[:, k, 0:width], in0=xin[:, b % 2, k, 0:width],
                                                   scalar=gain[:, k:k + 1], in1=rs[:, 0:width],
                                                   op0=ALU.mult, op1=ALU.mult).then_inc(s_xn, 1)
                for k in range(KC):
                    dve.wait_ge(s_xhi, KC * b + k + 1)
                    nc.vector.tensor_tensor(xlo[:, b % 2, k, 0:width], xn[:, k, 0:width],
                                            xhi[:, b % 2, k, 0:width].bitcast(F32), ALU.subtract).then_inc(s_xlo, 1)

            def rotate(b, t, width):
                u = NROPE * b + t
                src = rq[:, t % 2] if isq else krin[:, b % 2]
                dve.wait_ge(s_perm, u + 1)
                if u >= 2:
                    dve.wait_ge(s_rst[u % 2], 16 * (u // 2))
                nc.vector.tensor_tensor(t1[:, 0:width], src[:, 0:width], cs[:, b % 2, 0, 0:width], ALU.mult)
                link(nc.vector.tensor_tensor(t2[:, 0:width], ps[:, PERM, 0:width], cs[:, b % 2, 1, 0:width], ALU.mult))
                nc.vector.tensor_tensor(rob[:, u % 2, 0:width], t1[:, 0:width], t2[:, 0:width],
                                        ALU.add).then_inc(s_rope, 1)

            dve.wait_ge(s_gain, 16)
            norm(0, BLK)
            scale_done = False
            for n in range(NW):
                dve.wait_ge(s_whi, n + 1)
                nc.vector.tensor_tensor(wlo[:, :, n * BLK:(n + 1) * BLK], wst[:, n % 2],
                                        whi[:, :, n * BLK:(n + 1) * BLK].bitcast(F32), ALU.subtract).then_inc(s_wlo, 1)
                if n == 0:
                    scale(0, BLK)
            for b, col, width in blocks:
                more = b + 1 < len(blocks)
                if more:
                    norm(b + 1, blocks[b + 1][2])
                for t in range(NROPE):
                    rotate(b, t, width)
                if more:
                    scale(b + 1, blocks[b + 1][2])

        @block.tensor
        def _(pe):
            def column_sum(b, width):
                pe.wait_ge(s_sum, b + 1)
                nc.tensor.matmul(ps[:, SUM, 0:width], net.ones[:], ssum[:, 0:width], start=True,
                                 stop=True).then_inc(s_ones, 1)

            def permute(b, t, width):
                u = NROPE * b + t
                src = rq[:, t % 2] if isq else krin[:, b % 2]
                if isq:
                    pe.wait_ge(s_rq, u + 1)
                else:
                    pe.wait_ge(s_x[b % 2], 16 * NLOAD * (b // 2 + 1))
                if u:
                    pe.wait_ge(s_rope, u)
                nc.tensor.matmul(ps[:, PERM, 0:width], net.perm[:], src[:, 0:width], start=True,
                                 stop=True).then_inc(s_perm, 1)

            column_sum(0, BLK)
            for b, col, width in blocks:
                r = b % 2
                pe.wait_ge(s_xlo, KC * (b + 1))
                for j, (what, t, n) in enumerate(outputs(width)):
                    o = NO * b + j
                    if o >= 4:
                        pe.wait_ge(s_ev, o - 3)
                    if b == 0:
                        cols = {"rope": t * P, "nope": NROPE * P + t * P, "key": t * P, "val": HEADS * P + n * BLK}[what]
                        pe.wait_ge(s_wlo, cols // BLK + 1)
                    for k in range(KC):
                        first, last = k == 0, k == KC - 1
                        if what == "val":
                            wcol = slice(HEADS * P + n * BLK, HEADS * P + (n + 1) * BLK)
                            tok = slice(t * P, (t + 1) * P)
                            mm = split3(nc, ps[:, o % 4], xhi[:, r, k, tok], xlo[:, r, k, tok],
                                        whi[:, k, wcol], wlo[:, k, wcol], first, last)
                        else:
                            w0 = t * P + (NROPE * P if what == "nope" else 0)
                            mm = split3(nc, ps[:, o % 4, 0:width], whi[:, k, w0:w0 + P], wlo[:, k, w0:w0 + P],
                                        xhi[:, r, k, 0:width], xlo[:, r, k, 0:width], first, last)
                    mm.then_inc(s_out, 1)
                    if j == 1 and b + 1 < len(blocks):
                        column_sum(b + 1, blocks[b + 1][2])
                    if 1 <= j <= NROPE:
                        permute(b, j - 1, width)


def attention(nc, net):
    QT = BLK // P
    NBH = SEQ // BLK
    slots = list(range(NKT // 2)) + ["den"] + list(range(NKT // 2, NKT))
    cuts = [0, 5, 10, 14, SLOTS]
    TAIL = 2
    KEARLY = 2
    with nc.cleanup_on_exit(), ExitStack() as st:
        sb = lambda n, s, d=F32: st.enter_context(nc.sbuf_tensor("at_" + n, s, d))
        prob = sb("prob", [P, 2, QT, TOK])
        kst = sb("kst", [P, TOK])
        vst = sb("vst", [P, NKT, VDIM])
        khi, klo = sb("khi", [P, TOK], F32R), sb("klo", [P, TOK], F32R)
        vhi, vlo = sb("vhi", [P, NKT, VDIM], F32R), sb("vlo", [P, NKT, VDIM], F32R)
        krhi, krlo = sb("krhi", [P, TOK], F32R), sb("krlo", [P, TOK], F32R)
        qst, qrst = sb("qst", [P, 2, BLK]), sb("qrst", [P, 2, BLK])
        qhi, qlo = sb("qhi", [P, 2, BLK], F32R), sb("qlo", [P, 2, BLK], F32R)
        qr = sb("qr", [P, 2, BLK], F32R)
        pthi, ptlo = sb("pthi", [P, 3, BLK], F32R), sb("ptlo", [P, 3, BLK], F32R)
        mx = sb("mx", [P, 2, 8])
        nmax = sb("nmax", [P, 2])
        lsum = sb("lsum", [P, 2, 8])
        rl = sb("rl", [P, 2])
        dg = sb("dg", [P, 2, BLK])
        den = sb("den", [P, BLK])
        gst = sb("gst", [P, 2, BLK])
        gden = sb("gden", [P, BLK])
        og = sb("og", [P, 2, BLK])
        wmod = sb("wmod", [P, 2, KD, P])
        gp = sb("gp", [P, 2 * KD])
        gpT = sb("gpT", [2 * KD, P])
        S = st.enter_context(nc.psum_tensor("at_S", [P, NCHUNK, BLK], F32))
        T = st.enter_context(nc.psum_tensor("at_T", [P, 2, BLK], F32))
        O = st.enter_context(nc.psum_tensor("at_O", [P, BLK], F32))
        MSTEPS = 3
        MCOL = TOK - (NCHUNK - 1) * BLK
        macc = S[:, NCHUNK - 1, MCOL:MCOL + MOD_LATER]
        assert MOD_LATER == HEADS * NBH
        s_q = net.sems("at_q_in", 2)
        s_g = net.sems("at_g_in", 2)
        s_ogst = net.sems("at_og_stored", 2)
        s_wmod = net.sems("at_wmod_in", 2)
        s_mused, s_mprod, s_mstep, s_mod, s_amul, s_gp, s_gpT, s_row, s_rowst = (
            net.sem("at_" + n) for n in ("mod_used", "mod_prod", "mod_step", "mod", "amul", "gp", "gpt", "row", "row_stored"))
        (s_k, s_v, s_krin, s_krhi, s_kr, s_khi, s_klo, s_vhi, s_vlo, s_qhi, s_qlo, s_qk, s_mx, s_nmax, s_exp, s_rl, s_dg,
         s_tr, s_hi, s_lo, s_mm, s_gden, s_og, s_recip) = (net.sem("at_" + n) for n in (
             "k_in", "v_in", "kr_in", "krhi", "kr", "khi", "klo", "vhi", "vlo", "qhi", "qlo", "qk", "mx", "nmax", "exp",
             "rl", "dg", "tr", "hi", "lo", "mm", "gden", "og", "recip"))
        VC = 3
        KPV = NKT // VC
        block = st.enter_context(nc.Block())

        def index(h, j):
            return h * NBH + j

        def head1(t, h, *rest):
            return t[bass.ds(h, 1)] if not isinstance(h, int) else t[h:h + 1]

        def load_q(sp, h, j):
            h, j, r = h + j // NBH, j % NBH, j % 2
            cols = slice(j * BLK, (j + 1) * BLK)
            sp.dma_start(qst[:, r], head1(net.qn, h)[:, :, cols].rearrange("a p n -> p (a n)")).then_inc(s_q[r], 16)
            for half in range(2):
                sp.dma_start(qrst[half * ROPE:(half + 1) * ROPE, r],
                             head1(net.qr_heads, h)[:, :, cols].rearrange("a p n -> p (a n)")).then_inc(s_q[r], 16)

        def load_gate(sp, h, j):
            sp.dma_start(gst[:, j % 2], head1(net.gate0, h)[:, :, j * BLK:(j + 1) * BLK].rearrange("a p n -> p (a n)")
                         ).then_inc(s_g[j % 2], 16)

        def load_k(sp, h):
            sp.dma_start(kst[:], head1(net.kn, h).rearrange("a p n -> p (a n)")).then_inc(s_k, 16)

        def load_v(sp, h):
            if isinstance(h, int):
                src = net.v[:, :, h * VDIM:(h + 1) * VDIM]
            else:
                src = net.v[:, :, bass.ds(h * VDIM, VDIM)]
            sp.dma_start(vst[:], src.rearrange("t p d -> p t d")).then_inc(s_v, 16)

        def load_mod(sp, b, r):
            src = net.w_mod[bass.ds(b + MOD_FIRST, 1)] if not isinstance(b, int) else net.w_mod[
                MOD_FIRST + b:MOD_FIRST + b + 1]
            sp.dma_start(wmod[:, r], src.rearrange("a p k c -> p (a k) c")).then_inc(s_wmod[r], 16)

        @block.sync
        def _(sp):
            load_q(sp, 0, 0)
            load_k(sp, 0)
            sp.dma_start(prob[:, 1, 0], net.kr).then_inc(s_krin, 16)
            load_v(sp, 0)
            load_q(sp, 0, 1)
            load_gate(sp, 0, 0)
            for r in range(2):
                load_mod(sp, r, r)
            sp.wait_ge(s_qlo, 1)
            load_q(sp, 0, 2)

            def phase(h, j, last):
                b = index(h, j)
                if not last and j == 0:
                    sp.wait_ge(s_klo, h * NCHUNK + NCHUNK)
                    load_k(sp, h + 1)
                if not last and j == 1:
                    sp.wait_ge(s_vlo, h * VC + VC)
                    load_v(sp, h + 1)
                if not last or j + 1 < NBH:
                    if not isinstance(h, int) or h or j:
                        sp.wait_ge(s_gden, b)
                    nh, nj = (h, j + 1) if j + 1 < NBH else (h + 1, 0)
                    load_gate(sp, nh, nj)
                if not last or j + 3 < NBH:
                    sp.wait_ge(s_qlo, b + 2)
                    load_q(sp, h, j + 3)
                if not last or j + 2 < NBH:
                    sp.wait_ge(s_mused, b + 1)
                    load_mod(sp, b + 2, j % 2)

            for j in range(NBH):
                phase(0, j, False)
            with sp.Fori(1, HEADS - 1) as h:
                for j in range(NBH):
                    phase(h, j, False)
            for j in range(NBH):
                phase(HEADS - 1, j, True)
            sp.wait_ge(s_row, 1)
            sp.dma_start(net.gp_row, gpT[:]).then_inc(s_rowst, 16)
            sp.wait_ge(s_rowst, 16)

        @block.tensor
        def _(pe):
            def scores(h, j, i, c):
                b = index(h, j)
                t = b * QT + i
                if i == 0 and c == 0:
                    pe.wait_ge(s_qlo, b + 1)
                if j == 0 and i == 0:
                    pe.wait_ge(s_klo, h * NCHUNK + (c + 1))
                if not (isinstance(t, int) and t == 0):
                    pe.wait_ge(s_exp, (t - 1) * NCHUNK + (c + 1))
                r, q, k = j % 2, slice(i * P, (i + 1) * P), chunk(c)
                out = S[:, c, 0:k.stop - k.start]
                nc.tensor.matmul(out, qhi[:, r, q], khi[:, k], start=True, stop=False)
                nc.tensor.matmul(out, qhi[:, r, q], klo[:, k], start=False, stop=False)
                nc.tensor.matmul(out, qlo[:, r, q], khi[:, k], start=False, stop=False)
                nc.tensor.matmul(out, qr[:, r, q], krhi[:, k], start=False, stop=False)
                nc.tensor.matmul(out, qr[:, r, q], krlo[:, k], start=False, stop=True).then_inc(s_qk, 1)

            def transposes(h, j, n):
                b = index(h, j)
                m = n + SLOTS * j
                if not (isinstance(h, int) and h == 0 and m < 2):
                    prev = (n - 2) % SLOTS
                    if slots[prev] == "den":
                        pe.wait_ge(s_hi, h * (SLOTS * NBH) + (m - 1))
                    else:
                        before = sum(1 for x in range(n - 1 if n >= 2 else SLOTS + n - 1) if slots[x] != "den")
                        pe.wait_ge(s_lo, (b if n >= 2 else b - 1) * NKT + before)
                out = T[:, m % 2]
                kt = slots[n]
                if kt == "den":
                    pe.wait_ge(s_dg, b * QT + QT)
                    for i in range(QT):
                        mm = nc.tensor.matmul(out[:, i * P:(i + 1) * P], net.ones[:], dg[:, j % 2, i * P:(i + 1) * P],
                                              start=True, stop=True)
                else:
                    if kt % (BLK // P) == 0:
                        pe.wait_ge(s_exp, b * (QT * NCHUNK) + ((QT - 1) * NCHUNK + kt // (BLK // P) + 1))
                    for i in range(QT):
                        mm = nc.tensor.transpose(out[:, i * P:(i + 1) * P], prob[:, j % 2, i, kt * P:(kt + 1) * P],
                                                 net.ident[:])
                mm.then_inc(s_tr, 1)

            def values(h, j, n):
                kt = slots[n]
                if kt == "den":
                    return
                b = index(h, j)
                if j == 0 and kt % KPV == 0:
                    pe.wait_ge(s_vlo, h * VC + (kt // KPV + 1))
                if kt == 0 and not (isinstance(b, int) and b == 0):
                    pe.wait_ge(s_og, b)
                pe.wait_ge(s_lo, b * NKT + (kt + 1))
                r = kt % 3
                split3(nc, O[:], vhi[:, kt], vlo[:, kt], pthi[:, r], ptlo[:, r], kt == 0,
                       kt == NKT - 1).then_inc(s_mm, 1)

            def modulation_tile(h, j):
                b = index(h, j)
                r = j % 2
                if isinstance(b, int):
                    pe.wait_ge(s_exp, min((b + 1) * QT + 1, HEADS * NBH * QT) * NCHUNK)
                    col = slice(b, b + 1)
                else:
                    pe.wait_ge(s_exp, ((b + 1) * QT + 1) * NCHUNK)
                    col = bass.ds(b, 1)
                pe.wait_ge(s_mprod, b + 1)
                nc.tensor.matmul(macc[:, col], wmod[:, r, 0], net.ones[:, 0:1], start=True,
                                 stop=True).then_inc(s_mused, 1)

            def phase(h, j, with_scores=True):
                nh, nj = (h, j + 1) if j + 1 < NBH else (h + 1, 0)
                for i in range(QT):
                    ns = list(range(cuts[i], cuts[i + 1]))
                    for c in range(NCHUNK):
                        if i == 1 and c == NCHUNK - 1:
                            modulation_tile(h, j)
                        if with_scores:
                            scores(nh, nj, i, c)
                        if c < len(ns) - TAIL:
                            step(h, j, ns[c])
                        if i == 0 and c == TAIL + 1:
                            values(h, j, 0)
                    for n in ns[-TAIL:]:
                        step(h, j, n)

            def step(h, j, n):
                transposes(h, j, n)
                if n > 2:
                    values(h, j, n - 2)
                elif n < 2 and not (isinstance(h, int) and h == 0 and j == 0):
                    values(*((h, j - 1) if j else (h - 1, NBH - 1)), SLOTS - 2 + n)

            pe.wait_ge(s_kr, 1)
            for i in range(QT):
                for c in range(NCHUNK):
                    scores(0, 0, i, c)
            for j in range(NBH):
                phase(0, j)
            with pe.Fori(1, HEADS - 1) as h:
                for j in range(NBH):
                    phase(h, j)
            for j in range(NBH):
                phase(HEADS - 1, j, j + 1 < NBH)
            for n in (SLOTS - 2, SLOTS - 1):
                values(HEADS - 1, NBH - 1, n)
            pe.wait_ge(s_gp, 2)
            nc.tensor.transpose(S[0:2 * KD, 0, 0:P], gp[:], net.ident[:]).then_inc(s_gpT, 1)

        @block.scalar
        def _(act):
            def k_high(h, c):
                act.wait_ge(s_k, h * 16 + 16)
                if not (isinstance(h, int) and h == 0):
                    act.wait_ge(s_qk, h * (NBH * QT * NCHUNK) - (NCHUNK - 1 - c))
                nc.scalar.activation(khi[:, chunk(c)], kst[:, chunk(c)], ACT.Copy).then_inc(s_khi, 1)

            def v_high(h, c):
                act.wait_ge(s_v, h * 16 + 16)
                if not (isinstance(h, int) and h == 0):
                    act.wait_ge(s_mm, h * (NBH * NKT) - (NKT - (c + 1) * KPV))
                nc.scalar.activation(vhi[:, c * KPV:(c + 1) * KPV], vst[:, c * KPV:(c + 1) * KPV],
                                     ACT.Copy).then_inc(s_vhi, 1)

            def q_high(h, j):
                h, j = h + j // NBH, j % NBH
                b, r = index(h, j), j % 2
                act.wait_ge(s_q[r], h * (48 * NBH // 2) + 48 * (j // 2 + 1))
                if not (isinstance(b, int) and b < 2):
                    act.wait_ge(s_qk, (b - 1) * (QT * NCHUNK))
                nc.scalar.activation(qhi[:, r], qst[:, r], ACT.Copy).then_inc(s_qhi, 1)
                nc.scalar.activation(qr[:, r], qrst[:, r], ACT.Copy).then_inc(s_qhi, 1)

            def exponential(h, j, i, c):
                b = index(h, j)
                t = b * QT + i
                if c == 0:
                    act.wait_ge(s_nmax, t + 1)
                    if not (isinstance(t, int) and t < 2):
                        act.wait_ge(s_rl, t - 1)
                    if i == 0 and not (isinstance(b, int) and b < 2):
                        act.wait_ge(s_tr, (b - 1) * SLOTS)
                k = chunk(c)
                nc.scalar.activation(prob[:, j % 2, i, k], S[:, c, 0:k.stop - k.start], ACT.Exp, scale=SCALE,
                                     bias=nmax[:, i % 2:i % 2 + 1],
                                     accum_out=lsum[:, i % 2, c:c + 1]).then_inc(s_exp, 1)

            def high(h, j, n):
                b = index(h, j)
                act.wait_ge(s_tr, h * (SLOTS * NBH) + (n + SLOTS * j + 1))
                kt = slots[n]
                if kt == "den":
                    if not (isinstance(b, int) and b == 0):
                        act.wait_ge(s_gden, b)
                    dst = den[:]
                else:
                    if not (isinstance(b, int) and b == 0 and kt < 3):
                        act.wait_ge(s_mm, b * NKT + (kt - 2))
                    dst = pthi[:, kt % 3]
                nc.scalar.activation(dst, T[:, (n + SLOTS * j) % 2], ACT.Copy).then_inc(s_hi, 1)

            def store_output(h, j):
                act.wait_ge(s_og, index(h, j) + 1)
                act.dma_start(head1(net.og, h)[:, :, j * BLK:(j + 1) * BLK].rearrange("a p n -> p (a n)"),
                              og[:, j % 2]).then_inc(s_ogst[j % 2], 16)

            def phase(h, j, last=False):
                nh, nj = (h, j + 1) if j + 1 < NBH else (h + 1, 0)
                with_scores = not last or j + 1 < NBH
                head_ends = j == NBH - 2 and not last
                for i in range(QT):
                    ns = list(range(cuts[i], cuts[i + 1]))
                    for c, n in enumerate(ns[:-TAIL]):
                        high(h, j, n)
                        if head_ends and i == QT - 1:
                            k_high(h + 1, c)
                        if c == 0:
                            if j == NBH - 1 and not last and i >= 2:
                                v_high(h + 1, i - 2)
                            if j == 0 and i == 1:
                                v_high(h, VC - 1)
                    if i == 1 and (not last or j + 2 < NBH):
                        q_high(h, j + 2)
                    if i == 1 and not (isinstance(h, int) and h == 0 and j == 0):
                        store_output(*((h, j - 1) if j else (h - 1, NBH - 1)))
                    if with_scores:
                        exponential(nh, nj, i, 0)
                    high(h, j, ns[-2])
                    if with_scores:
                        exponential(nh, nj, i, 1)
                        exponential(nh, nj, i, 2)
                    high(h, j, ns[-1])
                    if head_ends and i == QT - 1:
                        for c in range(len(ns) - TAIL, NCHUNK):
                            k_high(h + 1, c)
                    if with_scores:
                        exponential(nh, nj, i, 3)
                        exponential(nh, nj, i, 4)

            act.wait_ge(s_krin, 16)
            nc.scalar.activation(krhi[:], prob[:, 1, 0], ACT.Copy).then_inc(s_krhi, 1)
            q_high(0, 0)
            for c in range(NCHUNK):
                k_high(0, c)
            for i in range(QT):
                for c in range(NCHUNK):
                    exponential(0, 0, i, c)
                if i == 1:
                    q_high(0, 1)
            for c in range(VC - 1):
                v_high(0, c)
            for j in range(NBH):
                phase(0, j)
            with act.Fori(1, HEADS - 1) as h:
                for j in range(NBH):
                    phase(h, j)
            for j in range(NBH):
                phase(HEADS - 1, j, True)
            store_output(HEADS - 1, NBH - 1)
            for k in range(2):
                act.wait_ge(s_ogst[k], 16 * HEADS * NBH // 2)

        @block.vector
        def _(dve):
            def k_low(h, c):
                dve.wait_ge(s_khi, h * NCHUNK + (c + 1))
                nc.vector.tensor_tensor(klo[:, chunk(c)], kst[:, chunk(c)], khi[:, chunk(c)].bitcast(F32),
                                        ALU.subtract).then_inc(s_klo, 1)

            def v_low(h, c):
                dve.wait_ge(s_vhi, h * VC + (c + 1))
                v = slice(c * KPV, (c + 1) * KPV)
                nc.vector.tensor_tensor(vlo[:, v], vst[:, v], vhi[:, v].bitcast(F32), ALU.subtract).then_inc(s_vlo, 1)

            def q_low(h, j):
                h, j = h + j // NBH, j % NBH
                b, r = index(h, j), j % 2
                dve.wait_ge(s_qhi, b * 2 + 2)
                nc.vector.tensor_tensor(qlo[:, r], qst[:, r], qhi[:, r].bitcast(F32), ALU.subtract)
                nc.vector.tensor_tensor(qr[ROPE:P, r], qrst[ROPE:P, r], qr[ROPE:P, r].bitcast(F32),
                                        ALU.subtract).then_inc(s_qlo, 1)

            def maximum(h, j, i, c):
                t = index(h, j) * QT + i
                dve.wait_ge(s_qk, t * NCHUNK + (c + 1))
                k = chunk(c)
                nc.vector.tensor_reduce(mx[:, i % 2, c:c + 1], S[:, c, 0:k.stop - k.start], AXX,
                                        ALU.max).then_inc(s_mx, 1)

            def negated(h, j, i):
                t = index(h, j) * QT + i
                dve.wait_ge(s_mx, t * (NCHUNK + 1) + NCHUNK)
                nc.vector.tensor_reduce(mx[:, i % 2, 7:8], mx[:, i % 2, 0:NCHUNK], AXX, ALU.max).then_inc(s_mx, 1)
                dve.wait_ge(s_mx, (t + 1) * (NCHUNK + 1))
                if not (isinstance(t, int) and t < 2):
                    dve.wait_ge(s_exp, (t - 1) * NCHUNK)
                nc.vector.tensor_scalar(nmax[:, i % 2:i % 2 + 1], mx[:, i % 2, 7:8], -SCALE, None,
                                        ALU.mult).then_inc(s_nmax, 1)

            def denominator(h, j, i):
                b = index(h, j)
                t = b * QT + i
                dve.wait_ge(s_exp, (t + 1) * NCHUNK)
                nc.vector.tensor_reduce(lsum[:, i % 2, 7:8], lsum[:, i % 2, 0:NCHUNK], AXX, ALU.add).then_inc(s_rl, 1)
                dve.wait_ge(s_rl, t + 1)
                nc.vector.reciprocal(rl[:, i % 2:i % 2 + 1], lsum[:, i % 2, 7:8]).then_inc(s_recip, 1)
                dve.wait_ge(s_recip, t + 1)
                if i == 0 and not (isinstance(b, int) and b < 2):
                    dve.wait_ge(s_tr, (b - 1) * SLOTS)
                nc.vector.tensor_scalar(dg[:, j % 2, i * P:(i + 1) * P], net.ident[:], rl[:, i % 2:i % 2 + 1], None,
                                        ALU.mult).then_inc(s_dg, 1)

            def low(h, j, n):
                kt = slots[n]
                if kt == "den":
                    return
                dve.wait_ge(s_hi, h * (SLOTS * NBH) + (n + SLOTS * j + 1))
                nc.vector.tensor_tensor(ptlo[:, kt % 3], T[:, (n + SLOTS * j) % 2], pthi[:, kt % 3].bitcast(F32),
                                        ALU.subtract).then_inc(s_lo, 1)

            def output(h, j):
                b = index(h, j)
                dve.wait_ge(s_mm, b * NKT + NKT)
                dve.wait_ge(s_gden, b + 1)
                if not (isinstance(h, int) and h == 0 and j < 2):
                    dve.wait_ge(s_ogst[j % 2], h * (16 * NBH // 2) + 16 * (j // 2))
                nc.vector.tensor_tensor(og[:, j % 2], O[:], gden[:], ALU.mult).then_inc(s_og, 1)

            def phase(h, j, last=False):
                nh, nj = (h, j + 1) if j + 1 < NBH else (h + 1, 0)
                with_scores = not last or j + 1 < NBH
                for i in range(QT):
                    ns = list(range(cuts[i], cuts[i + 1]))
                    for c in range(NCHUNK):
                        if with_scores:
                            maximum(nh, nj, i, c)
                        if c < len(ns) - TAIL:
                            low(h, j, ns[c])
                        if j == NBH - 2 and not last and i == QT - 1 and c < KEARLY:
                            k_low(h + 1, c)
                        if c == 0:
                            if j == NBH - 1 and not last and i >= 2:
                                v_low(h + 1, i - 2)
                            if j == 0 and i == 1:
                                v_low(h, VC - 1)
                        if c == 1:
                            if i:
                                if with_scores:
                                    denominator(nh, nj, i - 1)
                            else:
                                if not (isinstance(h, int) and h == 0 and j == 0):
                                    output(*((h, j - 1) if j else (h - 1, NBH - 1)))
                                denominator(h, j, QT - 1)
                        if j == NBH - 1 and with_scores and i == 0 and c == 0:
                            k_low(h + 1, NCHUNK - 1)
                    if with_scores:
                        negated(nh, nj, i)
                    if i == 1 and (not last or j + 2 < NBH):
                        q_low(h, j + 2)
                    for n in ns[-TAIL:]:
                        low(h, j, n)
                    if j == NBH - 2 and not last and i == QT - 1:
                        for c in range(KEARLY, NCHUNK - 1):
                            k_low(h + 1, c)

            dve.wait_ge(s_krhi, 1)
            nc.vector.tensor_tensor(krlo[:], prob[:, 1, 0], krhi[:].bitcast(F32), ALU.subtract).then_inc(s_kr, 1)
            q_low(0, 0)
            for c in range(NCHUNK):
                k_low(0, c)
            for i in range(QT):
                for c in range(NCHUNK):
                    maximum(0, 0, i, c)
                negated(0, 0, i)
                if i:
                    denominator(0, 0, i - 1)
                if i == 1:
                    q_low(0, 1)
            for c in range(VC - 1):
                v_low(0, c)
            for j in range(NBH):
                phase(0, j)
            with dve.Fori(1, HEADS - 1) as h:
                for j in range(NBH):
                    phase(h, j)
            for j in range(NBH):
                phase(HEADS - 1, j, True)
            dve.wait_ge(s_mused, MOD_LATER)
            nc.vector.tensor_tensor(net.mod[:, MOD_FIRST:MOD_TILES, 0], macc, net.bm[:, MOD_FIRST:MOD_TILES],
                                    ALU.add).then_inc(s_mod, 1)
            dve.wait_ge(s_mod, 1)
            scale_rows(nc, net, 1, 1).then_inc(s_amul, 1)
            for l in range(2):
                gate = 3 * KD * l + 2 * KD
                nc.vector.tensor_tensor(gp[:, l * KD:(l + 1) * KD], net.mod[:, gate:gate + KD, 0], net.gpost[:, l],
                                        ALU.mult).then_inc(s_gp, 1)
            output(HEADS - 1, NBH - 1)
            dve.wait_ge(s_gpT, 1)
            nc.vector.tensor_copy(gpT[:], S[0:2 * KD, 0, 0:P]).then_inc(s_row, 1)

        @block.gpsimd
        def _(pool):
            def gate(h, j):
                b = index(h, j)
                pool.wait_ge(s_hi, h * (SLOTS * NBH) + (slots.index("den") + 1 + SLOTS * j))
                pool.wait_ge(s_g[j % 2], h * (16 * NBH // 2) + 16 * (j // 2 + 1))
                if not (isinstance(b, int) and b == 0):
                    pool.wait_ge(s_og, b)
                nc.gpsimd.tensor_tensor(gden[:], den[:], gst[:, j % 2], ALU.mult).then_inc(s_gden, 1)

            def modulation_part(h, j):
                b, r = index(h, j), j % 2
                pool.wait_ge(s_wmod[r], h * (16 * NBH // 2) + 16 * (j // 2 + 1))
                link = Chain(pool, s_mstep, b * MSTEPS)
                link(nc.gpsimd.tensor_tensor(wmod[:, r], wmod[:, r], net.cc[:, :, 0:1].to_broadcast([P, KD, P]),
                                             ALU.mult))
                for half in (4, 2):
                    link(nc.gpsimd.tensor_tensor(wmod[:, r, 0:half], wmod[:, r, 0:half],
                                                 wmod[:, r, half:2 * half], ALU.add))
                nc.gpsimd.tensor_tensor(wmod[:, r, 0], wmod[:, r, 0], wmod[:, r, 1], ALU.add).then_inc(s_mprod, 1)

            for j in range(NBH):
                modulation_part(0, j)
                gate(0, j)
            with pool.Fori(1, HEADS) as h:
                for j in range(NBH):
                    modulation_part(h, j)
                    gate(h, j)




def attn_out(nc, net):
    W = 256
    NB = SEQ // W
    TB = W // P
    with nc.cleanup_on_exit(), ExitStack() as st:
        sb = lambda n, s, d=F32: st.enter_context(nc.sbuf_tensor("ao_" + n, s, d))
        wst = sb("w", [P, KD, D])
        whi, wlo = sb("whi", [P, KD, D], F32R), sb("wlo", [P, KD, D], F32R)
        oin = sb("oin", [P, 2, KD, W])
        ohi, olo = sb("ohi", [P, 2, KD, W], F32R), sb("olo", [P, 2, KD, W], F32R)
        xt = sb("x", [P, 2 * TB, D])
        gp = sb("gp", [P, D])
        tmp = sb("tmp", [P, D])
        junk = sb("junk", [P, D])
        ob = sb("ob", [P, 2, D])
        ss, rs = sb("ss", [P, 4]), sb("rs", [P, 4])
        ps = st.enter_context(nc.psum_tensor("ao_ps", [P, 4, D], F32))
        s_w, s_o = net.sems("ao_w_in", KD), net.sems("ao_o_in", 2)
        s_x, s_st = net.sems("ao_x_in", 2 * TB), net.sems("ao_stored", 2)
        (s_gp, s_whi, s_wlo, s_ohi, s_olo, s_y, s_ss, s_rt, s_rs, s_tmp, s_x1) = (
            net.sem("ao_" + n) for n in ("gp", "whi", "wlo", "ohi", "olo", "y", "ss", "rt", "rs", "tmp", "x1"))
        block = st.enter_context(nc.Block())

        def nxt(i, r):
            return (i, 1) if r == 0 else (i + 1, 0)

        def loop(eng, body):
            body(0, False)
            with eng.Fori(1, NB // 2 - 1) as i:
                body(i, False)
            body(NB // 2 - 1, True)

        def load_o(sp, i, r):
            sp.dma_start(oin[:, r], net.og[:, :, bass.ds(i * (2 * W) + r * W, W)].rearrange("k p n -> p k n")
                         ).then_inc(s_o[r], 16)

        def load_x(sp, i, s):
            sp.dma_start(xt[:, s], net.x[bass.ds(i * (2 * W) + s * P, P), :]).then_inc(s_x[s], 16)

        @block.sync
        def _(sp):
            load_o(sp, 0, 0)
            for k in range(KD):
                sp.dma_start(wst[:, k], net.w_o0[:, k]).then_inc(s_w[k], 16)
            load_o(sp, 0, 1)
            sp.dma_start(gp[:], net.gp_flat[0:1, :].to_broadcast([P, D])).then_inc(s_gp, 16)
            for s in range(2 * TB):
                load_x(sp, 0, s)

            def body(i, last):
                for r in range(2):
                    if not last:
                        sp.wait_ge(s_olo, i * 2 + (r + 1))
                        load_o(sp, i + 1, r)
                    for s in range(TB * r, TB * r + TB):
                        sp.wait_ge(s_x1, i * 4 + (s + 1))
                        sp.dma_start(net.x1[bass.ds(i * (2 * W) + s * P, P), :], ob[:, s % 2]
                                     ).then_inc(s_st[s % 2], 16)
                        if not last:
                            load_x(sp, i + 1, s)

            loop(sp, body)
            for k in range(2):
                sp.wait_ge(s_st[k], 16 * SEQ // P // 2)

        def o_high(act, i, r):
            act.wait_ge(s_o[r], i * 16 + 16)
            if not isinstance(i, int) or i:
                act.wait_ge(s_y, i * 4 + TB * (r - 1))
            nc.scalar.activation(ohi[:, r], oin[:, r], ACT.Copy).then_inc(s_ohi, 1)

        @block.scalar
        def _(act):
            o_high(act, 0, 0)
            for k in range(KD):
                act.wait_ge(s_w[k], 16)
                nc.scalar.activation(whi[:, k], wst[:, k], ACT.Copy).then_inc(s_whi, 1)

            def body(i, last):
                for r in range(2):
                    if not (last and r):
                        o_high(act, *nxt(i, r))
                    for s in range(TB * r, TB * r + TB):
                        act.wait_ge(s_y, i * 4 + (s + 1))
                        if not isinstance(i, int) or i:
                            act.wait_ge(s_tmp, i * 4 + (s - 3))
                        nc.scalar.activation(junk[:], ps[:, s], ACT.Square, accum_out=ss[:, s:s + 1]).then_inc(s_ss, 1)
                        act.wait_ge(s_ss, i * 4 + (s + 1))
                        root_mean(nc, net, rs[:, s:s + 1], ss[:, s:s + 1], D).then_inc(s_rt, 1)

            loop(act, body)

        @block.vector
        def _(dve):
            def o_low(i, r):
                dve.wait_ge(s_ohi, i * 2 + (r + 1))
                nc.vector.tensor_tensor(olo[:, r], oin[:, r], ohi[:, r].bitcast(F32), ALU.subtract).then_inc(s_olo, 1)

            o_low(0, 0)
            for k in range(KD):
                dve.wait_ge(s_whi, k + 1)
                nc.vector.tensor_tensor(wlo[:, k], wst[:, k], whi[:, k].bitcast(F32),
                                        ALU.subtract).then_inc(s_wlo, 1)
            dve.wait_ge(s_gp, 16)

            def body(i, last):
                for r in range(2):
                    if not (last and r):
                        o_low(*nxt(i, r))
                    for s in range(TB * r, TB * r + TB):
                        dve.wait_ge(s_rt, i * 4 + (s + 1))
                        nc.vector.reciprocal(rs[:, s:s + 1], rs[:, s:s + 1]).then_inc(s_rs, 1)
                        dve.wait_ge(s_rs, i * 4 + (s + 1))
                        nc.vector.scalar_tensor_tensor(out=tmp[:], in0=ps[:, s], scalar=rs[:, s:s + 1], in1=gp[:],
                                                       op0=ALU.mult, op1=ALU.mult).then_inc(s_tmp, 1)
                        dve.wait_ge(s_tmp, i * 4 + (s + 1))
                        dve.wait_ge(s_x[s], i * 16 + 16)
                        if s >= 2 or not isinstance(i, int) or i:
                            dve.wait_ge(s_st[s % 2], i * 32 + 16 * (s // 2))
                        nc.vector.tensor_tensor(ob[:, s % 2], tmp[:], xt[:, s], ALU.add).then_inc(s_x1, 1)

            loop(dve, body)

        @block.tensor
        def _(pe):
            def body(i, last):
                for r in range(2):
                    pe.wait_ge(s_olo, i * 2 + (r + 1))
                    for s in range(TB * r, TB * r + TB):
                        if not isinstance(i, int) or i:
                            pe.wait_ge(s_tmp, i * 4 + (s - 3))
                        tok = slice((s % TB) * P, (s % TB + 1) * P)
                        for n in range(2):
                            c = slice(n * BLK, (n + 1) * BLK)
                            for k in range(KD):
                                if isinstance(i, int) and i == 0 and s == 0 and n == 0:
                                    pe.wait_ge(s_wlo, k + 1)
                                mm = split3(nc, ps[:, s, c], ohi[:, r, k, tok], olo[:, r, k, tok],
                                            whi[:, k, c], wlo[:, k, c], k == 0, k == KD - 1)
                        mm.then_inc(s_y, 1)

            loop(pe, body)


def conv_in(nc, net, hhi, hlo):
    GROUPS = D // P
    CH = P // CCH
    with nc.cleanup_on_exit(), ExitStack() as st:
        sb = lambda n, s, d=F32: st.enter_context(nc.sbuf_tensor("ci_" + n, s, d))
        wst = sb("w", [P, 3, D])
        whi, wlo = sb("whi", [P, 3, D], F32R), sb("wlo", [P, 3, D], F32R)
        sig = sb("sig", [P, 2, BLK])
        ub, gb = sb("ub", [P, 2, PHASES, BLK // PHASES]), sb("gb", [P, 2, PHASES, BLK // PHASES])
        raw = sb("raw", [P, 4, NCOL])
        HALO = OFFS // 2
        uhi, ulo = (sb(n, [P, 2, NCOL + 2 * HALO], F32R) for n in ("uhi", "ulo"))
        taps = sb("taps", [P, CH, OFFS * PHASES])
        thi, tlo = sb("thi", [P, CH, OFFS * PHASES], F32R), sb("tlo", [P, CH, OFFS * PHASES])
        bhi, blo = (sb(n, [P, 2, OFFS, CCH, PHASES], F32R) for n in ("bhi", "blo"))
        mask, bdw = sb("mask", [P, CCH]), sb("bdw", [P, GROUPS * CH])
        zb = sb("zb", [P, 2, NCOL])
        ps = st.enter_context(nc.psum_tensor("ci_ps", [P, 8, BLK], F32))
        s_w = net.sems("ci_w_in", 3)
        s_ust, s_gst, s_zst = net.sems("ci_u_stored", 2), net.sems("ci_g_stored", 2), net.sems("ci_z_stored", 2)
        s_raw = net.sems("ci_raw_in", 4)
        (s_const, s_pad, s_taps, s_whi, s_wlo, s_ab, s_g, s_sig, s_mul, s_thi, s_tlo, s_uhi, s_ulo, s_bhi, s_blo, s_cv,
         s_z) = (net.sem("ci_" + n) for n in (
             "const", "pad", "taps", "whi", "wlo", "ab", "g", "sig", "mul", "thi", "tlo", "uhi", "ulo", "bhi", "blo",
             "cv", "z"))
        block = st.enter_context(nc.Block())
        B, A, G = range(3)

        def banded(t):
            return (t.rearrange("p (j f) -> p j f", j=OFFS).unsqueeze(2).to_broadcast([P, OFFS, CCH, PHASES]),
                    mask[:].unsqueeze(1).unsqueeze(3).to_broadcast([P, OFFS, CCH, PHASES]))

        def loop(eng, body):
            body(0, True, False)
            with eng.Fori(1, GROUPS - 1) as g:
                body(g, False, False)
            body(GROUPS - 1, False, True)

        def load_w(sp, g, s):
            sp.dma_start(wst[:, s], net.cv_w_in[bass.ds(g * 3 + s, 1)].rearrange("a p n -> p (a n)")
                         ).then_inc(s_w[s], 16)

        def columns(dram, g, b):
            return dram[bass.ds(g, 1), :, :, b * (BLK // PHASES):(b + 1) * (BLK // PHASES)].rearrange(
                "a c s n -> c (a s) n")

        def load_u(sp, g, q):
            sp.dma_start(raw[:, q % 4], net.u_chunks[bass.ds(g * CH + q, 1)].rearrange("a p n -> p (a n)")
                         ).then_inc(s_raw[q % 4], 16)

        @block.sync
        def _(sp):
            for s in range(3):
                load_w(sp, 0, s)
            sp.dma_start(mask[:], net.mask_in).then_inc(s_const, 16)
            sp.dma_start(bdw[:], net.b_dw).then_inc(s_const, 16)

            def body(g, first, last):
                if not first:
                    sp.wait_ge(s_tlo, g)
                sp.dma_start(taps[:], net.taps[bass.ds(g, 1)].rearrange("a p q t -> p (a q) t")).then_inc(s_taps, 16)
                if not last:
                    for s in (B, A, G):
                        sp.wait_ge(s_wlo, g * 3 + (s + 1))
                        load_w(sp, g + 1, s)
                for b in range(NBLK):
                    sp.wait_ge(s_mul, g * 8 + (b + 1))
                    sp.dma_start(columns(net.u_phases, g, b), ub[:, b % 2]).then_inc(s_ust[b % 2], 16)
                if not first:
                    sp.wait_ge(s_ulo, g * CH)
                for k in range(2):
                    sp.wait_ge(s_ust[k], g * 32 + 32)
                for q in range(4):
                    load_u(sp, g, q)
                for b in range(NBLK):
                    sp.wait_ge(s_mul, g * 8 + (NBLK + b + 1))
                    sp.dma_start(columns(net.gate1, g, b), gb[:, b % 2]).then_inc(s_gst[b % 2], 16)
                for q in range(CH):
                    if q + 4 < CH:
                        sp.wait_ge(s_ulo, g * CH + (q + 1))
                        load_u(sp, g, q + 4)
                    sp.wait_ge(s_z, g * CH + (q + 1))
                    sp.dma_start(net.z_chunks[bass.ds(g * CH + q, 1)].rearrange("a p n -> p (a n)"),
                                 zb[:, q % 2]).then_inc(s_zst[q % 2], 16)

            loop(sp, body)
            for k in range(2):
                sp.wait_ge(s_gst[k], 32 * GROUPS)
                sp.wait_ge(s_zst[k], 64 * GROUPS)

        def w_high(act, g, s, first):
            act.wait_ge(s_w[s], g * 16 + 16)
            if not first:
                if s == G:
                    act.wait_ge(s_g, g * NBLK)
                else:
                    act.wait_ge(s_ab, g * 2 * NBLK)
            nc.scalar.activation(whi[:, s], wst[:, s], ACT.Copy).then_inc(s_whi, 1)

        @block.scalar
        def _(act):
            for s in (B, A):
                w_high(act, 0, s, True)

            def sigmoid(g, n, src, first):
                if not first or n >= 2:
                    act.wait_ge(s_mul, g * 8 + (n - 1))
                nc.scalar.activation(sig[:, n % 2], src, ACT.Sigmoid).then_inc(s_sig, 1)

            def body(g, first, last):
                for b in range(NBLK):
                    act.wait_ge(s_ab, g * 8 + (2 * b + 1))
                    sigmoid(g, b, ps[:, 2 * b % 6], first)
                    if b == 0:
                        w_high(act, g, G, first)
                if not last:
                    for s in (B, A):
                        w_high(act, g + 1, s, False)
                act.wait_ge(s_taps, g * 16 + 16)
                if not first:
                    act.wait_ge(s_bhi, g * CH)
                nc.scalar.activation(thi[:], taps[:], ACT.Copy).then_inc(s_thi, 1)
                for b in range(NBLK):
                    act.wait_ge(s_g, g * 4 + (b + 1))
                    sigmoid(g, NBLK + b, ps[:, (8 + b) % 6], False)
                if first:
                    act.wait_ge(s_const, 32)
                    act.wait_ge(s_pad, 1)
                for q in range(CH + 1):
                    if q < CH:
                        act.wait_ge(s_raw[q % 4], g * 32 + 16 * (q // 4 + 1))
                        if not first or q >= 2:
                            act.wait_ge(s_cv, g * CH + (q - 1))
                        nc.scalar.activation(uhi[:, q % 2, HALO:HALO + NCOL], raw[:, q % 4], ACT.Copy).then_inc(s_uhi, 1)
                    if q:
                        c = q - 1
                        act.wait_ge(s_cv, g * CH + (c + 1))
                        if not first or c >= 2:
                            act.wait_ge(s_zst[c % 2], g * 64 + 16 * (c // 2))
                        nc.scalar.activation(zb[:, c % 2], ps[:, 6 + c % 2, 0:NCOL], ACT.Identity,
                                             bias=bdw[:, bass.ds(g * CH + c, 1)]).then_inc(s_z, 1)

            loop(act, body)

        @block.vector
        def _(dve):
            nc.vector.memset(uhi[:].bitcast(F32), 0.0)
            nc.vector.memset(ulo[:].bitcast(F32), 0.0).then_inc(s_pad, 1)

            def w_low(g, s):
                dve.wait_ge(s_whi, g * 3 + (s + 1))
                nc.vector.tensor_tensor(wlo[:, s], wst[:, s], whi[:, s].bitcast(F32), ALU.subtract).then_inc(s_wlo, 1)

            def product(g, n, dst, src, stored):
                dve.wait_ge(s_sig, g * 8 + (n + 1))
                if stored is not None:
                    dve.wait_ge(*stored)
                nc.vector.tensor_tensor(dst.rearrange("p s n -> p n s"), src.rearrange("p (n s) -> p n s", s=PHASES),
                                        sig[:, n % 2].rearrange("p (n s) -> p n s", s=PHASES),
                                        ALU.mult).then_inc(s_mul, 1)

            def body(g, first, last):
                for b in range(NBLK):
                    dve.wait_ge(s_ab, g * 8 + (2 * b + 2))
                    product(g, b, ub[:, b % 2], ps[:, (2 * b + 1) % 6],
                            None if first and b < 2 else (s_ust[b % 2], g * 32 + 16 * (b // 2)))
                    if b == 0:
                        w_low(g, G)
                if not last:
                    for s in (B, A):
                        w_low(g + 1, s)
                dve.wait_ge(s_thi, g + 1)
                if not first:
                    dve.wait_ge(s_blo, g * CH)
                nc.vector.tensor_tensor(tlo[:], taps[:], thi[:].bitcast(F32), ALU.subtract).then_inc(s_tlo, 1)
                for b in range(NBLK):
                    product(g, NBLK + b, gb[:, b % 2], ps[:, (8 + b) % 6],
                            None if first and b < 2 else (s_gst[b % 2], g * 32 + 16 * (b // 2)))
                if first:
                    dve.wait_ge(s_const, 32)
                for q in range(CH):
                    if not first or q >= 2:
                        dve.wait_ge(s_cv, g * CH + (q - 1))
                    nc.vector.tensor_tensor(bhi[:, q % 2], *banded(thi[:, q].bitcast(F32)), ALU.mult).then_inc(s_bhi, 1)
                    dve.wait_ge(s_uhi, g * CH + (q + 1))
                    nc.vector.tensor_tensor(ulo[:, q % 2, HALO:HALO + NCOL], raw[:, q % 4],
                                            uhi[:, q % 2, HALO:HALO + NCOL].bitcast(F32),
                                            ALU.subtract).then_inc(s_ulo, 1)

            for s in (B, A):
                w_low(0, s)
            loop(dve, body)

        @block.tensor
        def _(pe):
            def product(g, s, bank, b):
                for k in range(KD):
                    cols = slice(b * BLK, (b + 1) * BLK)
                    mm = split3(nc, ps[:, bank], whi[:, s, k * P:(k + 1) * P], wlo[:, s, k * P:(k + 1) * P],
                                hhi[:, k, cols], hlo[:, k, cols], k == 0, k == KD - 1)
                return mm

            def body(g, first, last):
                for b in range(NBLK):
                    for s in (B, A):
                        n = 2 * b + s
                        if b == 0:
                            pe.wait_ge(s_wlo, g * 3 + (s + 1))
                        if n >= 6:
                            if s == B:
                                pe.wait_ge(s_sig, g * 8 + (b - 3 + 1))
                            else:
                                pe.wait_ge(s_mul, g * 8 + (b - 3 + 1))
                        elif not first:
                            if n == 0:
                                pe.wait_ge(s_sig, (g - 1) * 8 + 4)
                            else:
                                pe.wait_ge(s_mul, (g - 1) * 8 + (n + 3))
                        product(g, s, n % 6, b).then_inc(s_ab, 1)
                pe.wait_ge(s_wlo, g * 3 + 3)
                for b in range(NBLK):
                    n = 8 + b
                    if (n - 6) % 2 == 0:
                        pe.wait_ge(s_sig, g * 8 + ((n - 6) // 2 + 1))
                    else:
                        pe.wait_ge(s_mul, g * 8 + ((n - 6) // 2 + 1))
                    product(g, G, n % 6, b).then_inc(s_g, 1)
                for q in range(CH):
                    pe.wait_ge(s_ulo, g * CH + (q + 1))
                    pe.wait_ge(s_bhi, g * CH + (q + 1))
                    pe.wait_ge(s_blo, g * CH + (q + 1))
                    if not first or q >= 2:
                        pe.wait_ge(s_z, g * CH + (q - 1))
                    for j in range(OFFS):
                        w = [t[:, q % 2, j].rearrange("p c f -> p (c f)") for t in (bhi, blo)]
                        mm = split3(nc, ps[:, 6 + q % 2, 0:NCOL], w[0], w[1], uhi[:, q % 2, j:j + NCOL],
                                    ulo[:, q % 2, j:j + NCOL], j == 0, j == OFFS - 1)
                    mm.then_inc(s_cv, 1)

            loop(pe, body)

        @block.gpsimd
        def _(pool):
            def body(g, first, last):
                if first:
                    pool.wait_ge(s_const, 32)
                pool.wait_ge(s_tlo, g + 1)
                for q in range(CH):
                    if not first or q >= 2:
                        pool.wait_ge(s_cv, g * CH + (q - 1))
                    nc.gpsimd.tensor_tensor(blo[:, q % 2], *banded(tlo[:, q]), ALU.mult).then_inc(s_blo, 1)

            loop(pool, body)


def conv_out(nc, net):
    W = NCOL
    TB = W // P
    NB = SEQ // W
    HK = KD // 2
    WR = 6
    with nc.cleanup_on_exit(), ExitStack() as st:
        sb = lambda n, s, d=F32: st.enter_context(nc.sbuf_tensor("co_" + n, s, d))
        wst = sb("w", [P, WR, D])
        whi, wlo = sb("whi", [P, KD, D], F32R), sb("wlo", [P, KD, D], F32R)
        z, gt = sb("z", [P, 2, KD, W]), sb("gt", [P, 2, KD, W])
        sq = sb("sq", [P, KD, W])
        zsum = sb("zsum", [P, HK, W])
        mu, rs = sb("mu", [P, W]), sb("rs", [P, W])
        v = sb("v", [P, KD, W])
        vhi, vlo = sb("vhi", [P, 2, KD, W], F32R), sb("vlo", [P, 2, KD, W], F32R)
        gln, bln = sb("gln", [P, KD]), sb("bln", [P, KD])
        xt = sb("x", [P, 2, D])
        gp, tmp, junk = sb("gp", [P, D]), sb("tmp", [P, D]), sb("junk", [P, D])
        ob = sb("ob", [P, 2, D])
        ss, rr = sb("ss", [P, 4]), sb("rr", [P, 4])
        ps = st.enter_context(nc.psum_tensor("co_ps", [P, 2, D], F32))
        pmu = st.enter_context(nc.psum_tensor("co_pmu", [P, BLK], F32))
        pvar = st.enter_context(nc.psum_tensor("co_pvar", [P, BLK], F32))
        s_w, s_z, s_gt = net.sems("co_w_in", WR), net.sems("co_z_in", 2), net.sems("co_gt_in", 2)
        s_x, s_st = net.sems("co_x_in", 2), net.sems("co_stored", 2)
        (s_const, s_whi, s_wlo, s_mean, s_mu, s_zc, s_sq, s_var, s_zn, s_sg, s_v, s_vg, s_vhi, s_vlo, s_y, s_ss, s_tmp,
         s_out, s_chain, s_rt, s_rs, s_mr, s_rr, s_zsum, s_add) = (net.sem("co_" + n) for n in (
             "const", "whi", "wlo", "mean", "mu", "zc", "sq", "var", "zn", "sg", "v", "vg", "vhi", "vlo", "y", "ss",
             "tmp", "out", "chain", "rt", "rs", "mr", "rr", "zsum", "add"))
        block = st.enter_context(nc.Block())

        def loop(eng, body):
            body(0, True, False)
            with eng.Fori(1, NB // 2 - 1) as i:
                body(i, False, False)
            body(NB // 2 - 1, False, True)

        def nxt(i, r):
            return (i, 1) if r == 0 else (i + 1, 0)

        def static(i, r):
            return isinstance(i, int) and 2 * i + r < 2

        def load_zg(sp, i, r):
            for dst, src, sem in ((z, net.z_phases, s_z), (gt, net.gate1, s_gt)):
                for half in range(2):
                    g = slice(half * KD // 2, (half + 1) * KD // 2)
                    sp.dma_start(dst[:, r, g], src[g, :, bass.ds(i * 2 + r, 1), :].rearrange("g p a n -> p (g a) n")
                                 ).then_inc(sem[r], 16)

        def rows(dram, i, r, u):
            return dram.rearrange("(n s) d -> s n d", s=PHASES)[bass.ds(i * 2 + r, 1), u * P:(u + 1) * P, :].rearrange(
                "a n d -> (a n) d")

        @block.sync
        def _(sp):
            def load_x(i, r, u):
                sp.dma_start(xt[:, u], rows(net.x1, i, r, u)).then_inc(s_x[u], 16)

            load_zg(sp, 0, 0)
            for dst, src in ((gln[:], net.g_ln), (bln[:], net.b_ln), (gp[:], net.gp_flat[1:2, :].to_broadcast([P, D]))):
                sp.dma_start(dst, src).then_inc(s_const, 16)
            for k in range(KD):
                if k >= WR:
                    sp.wait_ge(s_wlo, k - WR + 1)
                sp.dma_start(wst[:, k % WR], net.w_o1[:, k]).then_inc(s_w[k % WR], 16)
            load_zg(sp, 0, 1)
            for u in range(TB):
                load_x(0, 0, u)

            def body(i, first, last):
                for r in range(2):
                    if not last:
                        sp.wait_ge(s_vg, i * 4 + 2 * (r + 1))
                        load_zg(sp, i + 1, r)
                    for u in range(TB):
                        sp.wait_ge(s_out, i * 4 + (2 * r + u + 1))
                        sp.dma_start(rows(net.out, i, r, u), ob[:, u]).then_inc(s_st[u], 16)
                        if not (last and r):
                            load_x(*nxt(i, r), u)

            loop(sp, body)
            for u in range(2):
                sp.wait_ge(s_st[u], 16 * NB)

        @block.scalar
        def _(act):
            def mean(i, r):
                act.wait_ge(s_mean, i * 2 + (r + 1))
                nc.scalar.activation(mu[:], pmu[:, 0:W], ACT.Copy, scale=1.0 / D).then_inc(s_mu, 1)
                for half in range(2):
                    k = slice(half * HK, (half + 1) * HK)
                    act.wait_ge(s_zc, i * 4 + (2 * r + half + 1))
                    nc.scalar.activation(sq[:, k], z[:, r, k], ACT.Square).then_inc(s_sq, 1)

            def root(i, r):
                act.wait_ge(s_var, i * 2 + (r + 1))
                if not static(i, r) or r:
                    act.wait_ge(s_zn, i * 4 + 2 * r)
                root_mean(nc, net, rs[:], pvar[:, 0:W], D).then_inc(s_rt, 1)

            def silu_part(i, r):
                for k in range(KD):
                    if k % HK == 0:
                        act.wait_ge(s_zn, i * 4 + (2 * r + k // HK + 1))
                    nc.scalar.activation(sq[:, k], z[:, r, k], ACT.Sigmoid,
                                         scale=gln[:, k:k + 1], bias=bln[:, k:k + 1]).then_inc(s_sg, 1)

            def high(i, r):
                if not static(i, r):
                    act.wait_ge(s_y, i * 4 + 2 * (r - 1))
                for half in range(2):
                    k = slice(half * HK, (half + 1) * HK)
                    act.wait_ge(s_vg, i * 4 + (2 * r + half + 1))
                    nc.scalar.activation(vhi[:, r, k], v[:, k], ACT.Copy).then_inc(s_vhi, 1)

            def stat(i, r, u):
                s = 2 * r + u
                act.wait_ge(s_y, i * 4 + (s + 1))
                if not isinstance(i, int) or i:
                    act.wait_ge(s_tmp, i * 4 + (s - 3))
                nc.scalar.activation(junk[:], ps[:, u], ACT.Square, accum_out=ss[:, s:s + 1]).then_inc(s_ss, 1)
                act.wait_ge(s_ss, i * 4 + (s + 1))
                root_mean(nc, net, rr[:, s:s + 1], ss[:, s:s + 1], D).then_inc(s_mr, 1)

            act.wait_ge(s_const, 48)
            def weights_high(first, last):
                for k in range(first, last):
                    act.wait_ge(s_w[k % WR], 16 * (k // WR + 1))
                    nc.scalar.activation(whi[:, k], wst[:, k % WR], ACT.Copy).then_inc(s_whi, 1)

            mean(0, 0)
            weights_high(0, 3)
            root(0, 0)
            weights_high(3, 5)
            silu_part(0, 0)
            high(0, 0)
            weights_high(5, KD)
            mean(0, 1)

            def body(i, first, last):
                for r in range(2):
                    n = None if last and r else nxt(i, r)
                    if n:
                        root(*n)
                        silu_part(*n)
                    stat(i, r, 0)
                    if n:
                        high(*n)
                    if not last:
                        mean(i + 1, r)
                    stat(i, r, 1)

            loop(act, body)

        @block.vector
        def _(dve):
            def centre(i, r):
                dve.wait_ge(s_mu, i * 2 + (r + 1))
                dve.wait_ge(s_z[r], i * 32 + 32)
                for half in range(2):
                    k = slice(half * HK, (half + 1) * HK)
                    nc.vector.tensor_tensor(z[:, r, k], z[:, r, k], mu[:].unsqueeze(1).to_broadcast([P, HK, W]),
                                            ALU.subtract).then_inc(s_zc, 1)

            def normalise(i, r):
                link = Chain(dve, s_chain, i * (2 * KD) + r * KD)
                dve.wait_ge(s_rt, i * 2 + (r + 1))
                nc.vector.reciprocal(rs[:], rs[:]).then_inc(s_rs, 1)
                dve.wait_ge(s_rs, i * 2 + (r + 1))
                for half in range(2):
                    k = slice(half * HK, (half + 1) * HK)
                    nc.vector.tensor_tensor(z[:, r, k], z[:, r, k], rs[:].unsqueeze(1).to_broadcast([P, HK, W]),
                                            ALU.mult).then_inc(s_zn, 1)
                dve.wait_ge(s_zn, i * 4 + 2 * (r + 1))
                if not static(i, r) or r:
                    dve.wait_ge(s_vlo, i * 4 + 2 * r)
                for half in range(2):
                    for k in range(half * HK, (half + 1) * HK):
                        link(nc.vector.tensor_scalar(v[:, k], z[:, r, k], gln[:, k:k + 1], bln[:, k:k + 1],
                                                     ALU.mult, ALU.add))
                    k = slice(half * HK, (half + 1) * HK)
                    dve.wait_ge(s_sg, i * (2 * KD) + (KD * r + (half + 1) * HK))
                    nc.vector.tensor_tensor(v[:, k], v[:, k], sq[:, k], ALU.mult).then_inc(s_v, 1)

            def low(i, r):
                for half in range(2):
                    k = slice(half * HK, (half + 1) * HK)
                    dve.wait_ge(s_vhi, i * 4 + (2 * r + half + 1))
                    nc.vector.tensor_tensor(vlo[:, r, k], v[:, k], vhi[:, r, k].bitcast(F32),
                                            ALU.subtract).then_inc(s_vlo, 1)

            def residual(i, r, u):
                s = 2 * r + u
                dve.wait_ge(s_mr, i * 4 + (s + 1))
                nc.vector.reciprocal(rr[:, s:s + 1], rr[:, s:s + 1]).then_inc(s_rr, 1)
                dve.wait_ge(s_rr, i * 4 + (s + 1))
                nc.vector.scalar_tensor_tensor(out=tmp[:], in0=ps[:, u], scalar=rr[:, s:s + 1], in1=gp[:],
                                               op0=ALU.mult, op1=ALU.mult).then_inc(s_tmp, 1)
                dve.wait_ge(s_tmp, i * 4 + (s + 1))
                dve.wait_ge(s_x[u], i * 32 + 16 * (r + 1))
                if not (isinstance(i, int) and i == 0 and r == 0):
                    dve.wait_ge(s_st[u], i * 32 + 16 * r)
                nc.vector.tensor_tensor(ob[:, u], tmp[:], xt[:, u], ALU.add).then_inc(s_out, 1)

            dve.wait_ge(s_const, 48)
            def weights_low(first, last):
                for k in range(first, last):
                    dve.wait_ge(s_whi, k + 1)
                    nc.vector.tensor_tensor(wlo[:, k], wst[:, k % WR], whi[:, k].bitcast(F32),
                                            ALU.subtract).then_inc(s_wlo, 1)

            centre(0, 0)
            weights_low(0, 3)
            normalise(0, 0)
            weights_low(3, 5)
            low(0, 0)
            weights_low(5, KD)
            centre(0, 1)

            def body(i, first, last):
                for r in range(2):
                    n = None if last and r else nxt(i, r)
                    if n:
                        normalise(*n)
                    residual(i, r, 0)
                    if n:
                        low(*n)
                    if not last:
                        centre(i + 1, r)
                    residual(i, r, 1)

            loop(dve, body)

        @block.tensor
        def _(pe):
            def mean_sum(i, r):
                pe.wait_ge(s_zsum, i * 2 + (r + 1))
                nc.tensor.matmul(pmu[:, 0:W], net.ones[:], zsum[:, 0], start=True, stop=True).then_inc(s_mean, 1)

            def var_sum(i, r):
                for k in range(KD):
                    if k % HK == 0:
                        pe.wait_ge(s_sq, i * 4 + (2 * r + k // HK + 1))
                    mm = nc.tensor.matmul(pvar[:, 0:W], net.ones[:], sq[:, k], start=(k == 0), stop=(k == KD - 1))
                mm.then_inc(s_var, 1)

            mean_sum(0, 0)
            var_sum(0, 0)
            mean_sum(0, 1)

            def body(i, first, last):
                for r in range(2):
                    n = None if last and r else nxt(i, r)
                    for u in range(TB):
                        s = 2 * r + u
                        if not (first and r == 0):
                            pe.wait_ge(s_tmp, i * 4 + (s - 1))
                        tok = slice(u * P, (u + 1) * P)
                        for h in range(2):
                            c = slice(h * BLK, (h + 1) * BLK)
                            for k in range(KD):
                                if u == 0 and h == 0 and k % HK == 0:
                                    pe.wait_ge(s_vlo, i * 4 + (2 * r + k // HK + 1))
                                if first and s == 0 and h == 0:
                                    pe.wait_ge(s_wlo, k + 1)
                                mm = split3(nc, ps[:, u, c], vhi[:, r, k, tok], vlo[:, r, k, tok],
                                            whi[:, k, c], wlo[:, k, c], k == 0, k == KD - 1)
                            if u == 0 and h == 0 and n:
                                var_sum(*n)
                            if u == 1 and h == 0 and not last:
                                mean_sum(i + 1, r)
                        mm.then_inc(s_y, 1)

            loop(pe, body)

        @block.gpsimd
        def _(pool):
            def sums(i, r):
                pool.wait_ge(s_z[r], i * 32 + 32)
                if not static(i, r) or r:
                    pool.wait_ge(s_mean, i * 2 + r)
                link = Chain(pool, s_add, i * 4 + 2 * r)
                link(nc.gpsimd.tensor_tensor(zsum[:], z[:, r, 0:HK], z[:, r, HK:KD], ALU.add))
                link(nc.gpsimd.tensor_tensor(zsum[:, 0:HK // 2], zsum[:, 0:HK // 2], zsum[:, HK // 2:HK], ALU.add))
                nc.gpsimd.tensor_tensor(zsum[:, 0], zsum[:, 0], zsum[:, 1], ALU.add).then_inc(s_zsum, 1)

            def gate(i, r):
                pool.wait_ge(s_gt[r], i * 32 + 32)
                for half in range(2):
                    k = slice(half * HK, (half + 1) * HK)
                    pool.wait_ge(s_v, i * 4 + (2 * r + half + 1))
                    nc.gpsimd.tensor_tensor(v[:, k], v[:, k], gt[:, r, k], ALU.mult).then_inc(s_vg, 1)

            sums(0, 0)
            sums(0, 1)
            gate(0, 0)

            def body(i, first, last):
                for r in range(2):
                    n = None if last and r else nxt(i, r)
                    if not last:
                        sums(i + 1, r)
                    if n:
                        gate(*n)

            loop(pool, body)


def build(nc, io, out):
    with ExitStack() as stack:
        net = Net(nc, stack)
        sb = lambda n, s, d=F32: stack.enter_context(nc.sbuf_tensor(n, s, d))
        scratch = lambda n, s: nc.dram_tensor(n, s, F32, kind="Internal").ap()
        net.x, net.ctx, net.c_cols, net.out = io["x"], io["ctx"], io["c_cols"], out
        net.w_mod, net.b_mod, net.g_pre, net.g_post = io["w_mod"], io["b_mod"], io["g_pre"], io["g_post"]
        net.w_in, net.g_q, net.g_kv, net.w_uq, net.w_ukv = (io[n] for n in ("w_in", "g_q", "g_kv", "w_uq", "w_ukv"))
        net.w_o0, net.cv_w_in, net.taps, net.b_dw = io["w_o0"], io["cv_w_in"], io["taps"], io["b_dw"]
        net.g_ln, net.b_ln, net.w_o1 = io["g_ln"], io["b_ln"], io["w_o1"]
        net.ident_in, net.perm_in, net.mask_in, net.rope_tab = io["ident"], io["perm"], io["mask"], io["rope_tab"]

        net.raw = scratch("raw_latents", [KQ + KKV + 1, P, TOK])
        net.gate0 = scratch("silu_gate0", [HEADS, P, SEQ])
        net.qn = scratch("q_nope", [HEADS, P, SEQ])
        net.qr = scratch("q_rope", [HEADS // 2, P, SEQ])
        net.qr_heads = net.qr.rearrange("t (e p) n -> (t e) p n", e=2)
        net.kn = scratch("k_nope", [HEADS, P, TOK])
        net.kr = scratch("k_rope", [P, TOK])
        net.v = scratch("values", [NKT, P, HEADS * VDIM])
        net.og = scratch("attn_gated", [HEADS, P, SEQ])
        net.x1 = scratch("x1", [SEQ, D])
        net.u_phases = scratch("u_phases", [KD, P, PHASES, NCOL])
        net.u_chunks = net.u_phases.rearrange("g (q c) s n -> (g q) (c s) n", c=CCH)
        net.z_phases = scratch("z_phases", [KD, P, PHASES, NCOL])
        net.z_chunks = net.z_phases.rearrange("g (q c) s n -> (g q) (c s) n", c=CCH)
        net.gate1 = scratch("silu_gate1", [KD, P, PHASES, NCOL])
        net.gp_row = scratch("gate_rows", [2 * KD, P])
        net.gp_flat = net.gp_row.rearrange("(l k) p -> l (k p)", l=2)

        net.ident, net.perm, net.ones = sb("ident", [P, P]), sb("perm", [P, P]), sb("ones", [P, P])
        net.eps = sb("eps", [P, 1])
        net.mod = sb("mod", [P, 6 * KD, 2])
        net.amul = sb("amul", [P, 2, KD, 2])
        net.cc = sb("c_silu", [P, KD, 2])
        net.bm = sb("b_mod", [P, MOD_TILES])
        net.gpre, net.gpost = sb("g_pre", [P, 2, KD]), sb("g_post", [P, 2, KD])

        modulation(nc, net)
        with ExitStack() as st:
            hhi = st.enter_context(nc.sbuf_tensor("h0hi", [P, KD, TOK], F32R))
            hlo = st.enter_context(nc.sbuf_tensor("h0lo", [P, KD, TOK], F32R))
            hidden(nc, net, 0, net.x, net.ctx, hhi, hlo)
            in_proj(nc, net, hhi, hlo)
        latents(nc, net, "q")
        latents(nc, net, "kv")
        attention(nc, net)
        attn_out(nc, net)
        with ExitStack() as st:
            hhi = st.enter_context(nc.sbuf_tensor("h1hi", [P, KD, SEQ], F32R))
            hlo = st.enter_context(nc.sbuf_tensor("h1lo", [P, KD, SEQ], F32R))
            hidden(nc, net, 1, net.x1, None, hhi, hlo)
            conv_in(nc, net, hhi, hlo)
        conv_out(nc, net)


def constants():
    half = ROPE // 2
    freqs = (1.0 / (np.float32(10000.0) ** (np.arange(0, half, 2, dtype=np.float32) / np.float32(half)))).astype(
        np.float32)
    pos = np.arange(SEQ)
    ang = [(p.astype(np.float32)[None, :] * freqs[:, None]).astype(np.float32) for p in (pos // GRID_W, pos % GRID_W)]
    tab = np.zeros((2, ROPE, TOK), np.float32)
    tab[0, :, SEQ:] = 1.0
    for a in range(2):
        for h in range(2):
            rows = slice(a * half + h * half // 2, a * half + (h + 1) * half // 2)
            tab[0, rows, :SEQ], tab[1, rows, :SEQ] = np.cos(ang[a]), np.sin(ang[a])
    perm = np.zeros((P, P), np.float32)
    for m in range(P):
        if m % half < half // 2:
            perm[m + half // 2, m] = -1.0
        else:
            perm[m - half // 2, m] = 1.0
    mask = (np.arange(P)[:, None] // PHASES == np.arange(CCH)[None, :]).astype(np.float32)
    return {"rope_tab": np.tile(tab, (1, 2, 1)), "perm": perm, "mask": mask, "ident": np.eye(P, dtype=np.float32)}


def layout(i):
    a = {k: np.asarray(v) for k, v in i.items()}
    tiles = lambda w: w.reshape(w.shape[0] // P, P, -1, P).transpose(2, 1, 0, 3)
    cols = lambda w: w.reshape(-1, P).T
    out = {"x": a["x"][0], "ctx": a["ctx"][0]}
    out["c_cols"] = np.stack([cols(a["c"][0]), cols(a["c_ctx"])], axis=2)
    out["w_mod"] = np.concatenate([tiles(a["w_mod"][l]) for l in range(2)])
    out["b_mod"] = cols(a["b_mod"].reshape(-1))
    out["g_pre"], out["g_post"] = (a[n].reshape(2, KD, P).transpose(2, 0, 1) for n in ("g_pre", "g_post"))
    w = a["mla_w_in"][0]
    rope0 = QL + KVL
    w = np.concatenate([w[:, :rope0], w[:, rope0:rope0 + ROPE], w[:, rope0:rope0 + ROPE], w[:, rope0 + ROPE:]], axis=1)
    out["w_in"] = tiles(w).reshape(-1, P, D)
    out["g_q"], out["g_kv"] = cols(a["mla_g_q"][0]), cols(a["mla_g_kv"][0])
    w = a["mla_w_uq"][0].reshape(QL, HEADS, NOPE + ROPE)
    w = np.concatenate([w[:, :, NOPE:].reshape(QL, -1), w[:, :, :NOPE].reshape(QL, -1)], axis=1)
    out["w_uq"] = w.reshape(KQ, P, -1).transpose(1, 0, 2)
    w = a["mla_w_ukv"][0].reshape(KVL, HEADS, NOPE + VDIM)
    w = np.concatenate([w[:, :, :NOPE].reshape(KVL, -1), w[:, :, NOPE:].reshape(KVL, -1)], axis=1)
    out["w_ukv"] = w.reshape(KKV, P, -1).transpose(1, 0, 2)
    out["w_o0"], out["w_o1"] = (a[n][0].reshape(KD, P, D).transpose(1, 0, 2) for n in ("mla_w_o", "cv_w_o"))
    w = a["cv_w_in"][0].reshape(D, 3, KD, P)[:, [1, 0, 2]].transpose(0, 2, 1, 3).reshape(D, -1)
    out["cv_w_in"] = tiles(w).reshape(-1, P, D)
    dw = a["cv_w_dw"][0][:, 0, :]
    taps = np.zeros((D, PHASES, OFFS, PHASES), np.float32)
    for s in range(PHASES):
        for j in range(OFFS):
            for f in range(PHASES):
                t = PHASES * (j - OFFS // 2) + s - f + PAD
                if 0 <= t < CONV_K:
                    taps[:, s, j, f] = dw[t]
    out["taps"] = taps.reshape(KD, P // CCH, P, OFFS * PHASES).transpose(0, 2, 1, 3)
    out["b_dw"] = np.repeat(a["cv_b_dw"][0].reshape(-1, CCH), PHASES, axis=1).T
    out["g_ln"], out["b_ln"] = cols(a["cv_g_ln"][0]), cols(a["cv_b_ln"][0])
    out.update(constants())
    return {k: np.ascontiguousarray(v) for k, v in out.items()}


def kernel(**inputs):
    import concourse.bacc as bacc
    from concourse.bass_utils import run_bass_kernel_spmd

    arrays = layout(inputs)
    nc = bacc.Bacc("TRN2", target_bir_lowering=False, num_devices=1)
    io = {k: nc.dram_tensor(f"in_{k}", v.shape, F32, kind="ExternalInput").ap() for k, v in arrays.items()}
    out = nc.dram_tensor("out_x", (SEQ, D), F32, kind="ExternalOutput").ap()
    build(nc, io, out)
    r = run_bass_kernel_spmd(nc, [{f"in_{k}": v for k, v in arrays.items()}], core_ids=[0])
    return r.results[0]["out_x"].reshape(1, SEQ, D)
```
